# Optimizing a Trainium2 kernel written in Bass

```python
import jax, jax.numpy as jnp
from jax import lax
import numpy as np

D_MODEL = 2048
BATCH = 1
SEQ = 512
DEPTH = 1

D_A = D_MODEL // 2
D_B = D_MODEL // 2
A_HEADS = 8
A_EXPAND = D_A // A_HEADS
A_DV = D_A // A_HEADS
A_CHUNK = 64
B_HEADS = 16
B_KV_HEADS = 4
B_GROUP = B_HEADS // B_KV_HEADS
B_HEAD_DIM = D_B // B_HEADS
KV_DIM = B_KV_HEADS * B_HEAD_DIM
CMP_BLOCK = 32
CMP_STRIDE = 16
CMP_HIDDEN = 256
SLC_BLOCK = 64
SLC_TOP_N = 16
SLC_WEIGHTS = (1.0, 2.0, 2.0, 2.0, 1.0)
WINDOW = 512
Q_BLOCK = 128
ROPE_THETA = 500000.0
ROPE_DIM = B_HEAD_DIM // 4
D_FF = ((8 * D_MODEL // 3 + 255) // 256) * 256
EPS = 1e-6
NEG_INF = -1e30
FORCE_BONUS = 1e4
IN_SPLITS = (D_A, D_A, D_A, D_A, D_B, KV_DIM, KV_DIM, KV_DIM, KV_DIM, KV_DIM, KV_DIM, 3 * B_HEADS, D_MODEL, D_MODEL)
IN_COLS = 4 * D_A + D_B + 6 * KV_DIM + 3 * B_HEADS + 2 * D_MODEL

kernel_name = "hgrn2_nsa_parallel_hybrid_block"

def rms_norm(x, g):
    xf = x.astype(jnp.float32)
    y = xf * lax.rsqrt(jnp.mean(xf * xf, axis=-1, keepdims=True) + EPS)
    return (y * g.astype(jnp.float32)).astype(x.dtype)

def rope_partial(x, pos):
    half = ROPE_DIM // 2
    inv = jnp.float32(ROPE_THETA) ** (-jnp.arange(half, dtype=jnp.float32) * 2.0 / ROPE_DIM)
    ang = pos.astype(jnp.float32)[:, None] * inv[None, :]
    shape = (1, ang.shape[0]) + (1,) * (x.ndim - 3) + (half,)
    cos = jnp.cos(ang).reshape(shape).astype(x.dtype)
    sin = jnp.sin(ang).reshape(shape).astype(x.dtype)
    x1, x2, rest = x[..., :half], x[..., half:ROPE_DIM], x[..., ROPE_DIM:]
    return jnp.concatenate([x1 * cos - x2 * sin, x2 * cos + x1 * sin, rest], axis=-1)

def masked_softmax(s, mask):
    s = jnp.where(mask, s, NEG_INF)
    return jax.nn.softmax(s, axis=-1) * mask

def hgrn2_mixer(q, f_logit, inp, g, lb):
    b_, t_, _ = q.shape
    n_c = t_ // A_CHUNK
    f = lb + (1.0 - lb) * jax.nn.sigmoid(f_logit.astype(jnp.float32))
    log_f = jnp.log(f)
    k = 1.0 - f

    def to_chunks(a, d):
        return a.reshape(b_, n_c, A_CHUNK, A_HEADS, d).transpose(1, 0, 3, 2, 4)

    qc = to_chunks(q.astype(jnp.float32), A_EXPAND)
    kc = to_chunks(k, A_EXPAND)
    lfc = to_chunks(log_f, A_EXPAND)
    ic = to_chunks(inp.astype(jnp.float32), A_DV)
    tri = jnp.tril(jnp.ones((A_CHUNK, A_CHUNK), dtype=bool))

    def step(S, chunk):
        qq, kk, lf, ii = chunk
        bcum = jnp.cumsum(lf, axis=2)
        o_inter = jnp.einsum('bhte,bhev->bhtv', qq * jnp.exp(bcum), S)
        diff = bcum[:, :, :, None, :] - bcum[:, :, None, :, :]
        decay = jnp.where(tri[None, None, :, :, None], jnp.exp(jnp.minimum(diff, 0.0)), 0.0)
        att = jnp.einsum('bhtse,bhte,bhse->bhts', decay, qq, kk)
        o_intra = jnp.einsum('bhts,bhsv->bhtv', att, ii)
        b_end = bcum[:, :, -1, :]
        S_new = jnp.exp(b_end)[..., None] * S + jnp.einsum(
            'bhse,bhsv->bhev', kk * jnp.exp(b_end[:, :, None, :] - bcum), ii)
        return S_new, o_inter + o_intra

    S0 = jnp.zeros((b_, A_HEADS, A_EXPAND, A_DV), jnp.float32)
    _, o = lax.scan(step, S0, (qc, kc, lfc, ic))
    return o.transpose(1, 0, 3, 2, 4).reshape(b_, t_, A_HEADS, A_DV)

def compress(x, pe, w1, b1, w2, b2):
    b_, t_ = x.shape[0], x.shape[1]
    n_cmp = (t_ - CMP_BLOCK) // CMP_STRIDE + 1
    idx = jnp.arange(n_cmp)[:, None] * CMP_STRIDE + jnp.arange(CMP_BLOCK)[None, :]
    blocks = x[:, idx] + pe[None, None, :, None, :]
    flat = blocks.transpose(0, 1, 3, 2, 4).reshape(b_, n_cmp, B_KV_HEADS, CMP_BLOCK * B_HEAD_DIM)
    h = jax.nn.gelu(flat @ w1 + b1)
    return h @ w2 + b2, idx[:, -1]

def nsa_mixer(q, kc, vc, ks, vs, kw, vw, gate_logits, pe_k, w1k, b1k, w2k, b2k, pe_v, w1v, b1v, w2v, b2v):
    b_, t_, _ = q.shape
    pos = jnp.arange(t_)
    scale = B_HEAD_DIM ** -0.5
    qh = rope_partial(q.reshape(b_, t_, B_KV_HEADS, B_GROUP, B_HEAD_DIM), pos)
    gates = jax.nn.sigmoid(gate_logits.astype(jnp.float32)).reshape(b_, t_, B_KV_HEADS, B_GROUP, 3).astype(q.dtype)

    def heads(a):
        return a.reshape(b_, t_, B_KV_HEADS, B_HEAD_DIM)

    k_cmp, end_pos = compress(heads(kc), pe_k, w1k, b1k, w2k, b2k)
    v_cmp, _ = compress(heads(vc), pe_v, w1v, b1v, w2v, b2v)
    k_cmp = rope_partial(k_cmp, end_pos).transpose(0, 2, 1, 3)
    v_cmp = v_cmp.transpose(0, 2, 1, 3)
    n_cmp = k_cmp.shape[2]

    n_slc = t_ // SLC_BLOCK
    k_sel = min(SLC_TOP_N, n_slc)
    ks_blocks = rope_partial(heads(ks), pos).transpose(0, 2, 1, 3).reshape(b_, B_KV_HEADS, n_slc, SLC_BLOCK, B_HEAD_DIM)
    vs_blocks = heads(vs).transpose(0, 2, 1, 3).reshape(b_, B_KV_HEADS, n_slc, SLC_BLOCK, B_HEAD_DIM)
    gather_blocks = jax.vmap(jax.vmap(lambda blk, ix: blk[ix]))

    pad = ((0, 0), (0, 0), (WINDOW, 0), (0, 0))
    kw_pad = jnp.pad(rope_partial(heads(kw), pos).transpose(0, 2, 1, 3), pad)
    vw_pad = jnp.pad(heads(vw).transpose(0, 2, 1, 3), pad)

    blk_ids = jnp.arange(n_slc)
    right_pad = 4 * n_slc + 1 - (n_cmp + 1)
    ratio = SLC_BLOCK // CMP_STRIDE

    def block_fn(c):
        q0 = c * Q_BLOCK
        t = q0 + jnp.arange(Q_BLOCK)
        qc_ = lax.dynamic_slice_in_dim(qh, q0, Q_BLOCK, axis=1).astype(jnp.float32)
        gc = lax.dynamic_slice_in_dim(gates, q0, Q_BLOCK, axis=1)

        s_c = jnp.einsum('btkgd,bknd->bkgtn', qc_, k_cmp.astype(jnp.float32)) * scale
        p_c = masked_softmax(s_c, end_pos[None, :] <= t[:, None])
        o_cmp = jnp.einsum('bkgtn,bknd->btkgd', p_c.astype(v_cmp.dtype), v_cmp)

        p_sum = jnp.pad(p_c.sum(axis=2), ((0, 0), (0, 0), (0, 0), (1, right_pad)))
        p_slc = sum(w * p_sum[..., o: o + ratio * n_slc: ratio] for o, w in enumerate(SLC_WEIGHTS))
        cur = t // SLC_BLOCK
        valid = blk_ids[None, :] * SLC_BLOCK <= t[:, None]
        forced = (blk_ids[None, :] == 0) | (blk_ids[None, :] == cur[:, None]) | (blk_ids[None, :] == cur[:, None] - 1)
        score = jnp.where(forced, FORCE_BONUS, jnp.where(valid, p_slc, NEG_INF))
        _, sel = lax.top_k(score, k_sel)
        sel_flat = sel.reshape(b_, B_KV_HEADS, Q_BLOCK * k_sel)
        kg = gather_blocks(ks_blocks, sel_flat).reshape(b_, B_KV_HEADS, Q_BLOCK, k_sel * SLC_BLOCK, B_HEAD_DIM)
        vg = gather_blocks(vs_blocks, sel_flat).reshape(b_, B_KV_HEADS, Q_BLOCK, k_sel * SLC_BLOCK, B_HEAD_DIM)
        pos_sel = (sel[..., None] * SLC_BLOCK + jnp.arange(SLC_BLOCK)).reshape(b_, B_KV_HEADS, Q_BLOCK, k_sel * SLC_BLOCK)
        s_s = jnp.einsum('btkgd,bktnd->bkgtn', qc_, kg.astype(jnp.float32)) * scale
        p_s = masked_softmax(s_s, (pos_sel <= t[None, None, :, None])[:, :, None])
        o_slc = jnp.einsum('bkgtn,bktnd->btkgd', p_s.astype(vg.dtype), vg)

        kwc = lax.dynamic_slice_in_dim(kw_pad, q0, WINDOW + Q_BLOCK, axis=2)
        vwc = lax.dynamic_slice_in_dim(vw_pad, q0, WINDOW + Q_BLOCK, axis=2)
        kpos = q0 - WINDOW + jnp.arange(WINDOW + Q_BLOCK)
        m_w = (kpos[None, :] <= t[:, None]) & (t[:, None] - kpos[None, :] < WINDOW) & (kpos[None, :] >= 0)
        s_w = jnp.einsum('btkgd,bknd->bkgtn', qc_, kwc.astype(jnp.float32)) * scale
        p_w = masked_softmax(s_w, m_w)
        o_win = jnp.einsum('bkgtn,bknd->btkgd', p_w.astype(vwc.dtype), vwc)

        o = gc[..., 0:1] * o_cmp + gc[..., 1:2] * o_slc + gc[..., 2:3] * o_win
        return o.reshape(b_, Q_BLOCK, D_B)

    out = lax.map(block_fn, jnp.arange(t_ // Q_BLOCK))
    return out.transpose(1, 0, 2, 3).reshape(b_, t_, D_B)

def hybrid_mixer(xn, w_in, lb, a_norm_g, pe_k, w1k, b1k, w2k, b2k, pe_v, w1v, b1v, w2v, b2v,
                 w_proj_a, w_proj_b, w_out):
    proj = xn @ w_in
    offsets = [int(o) for o in np.cumsum(IN_SPLITS)[:-1]]
    (qa, fa, ia, ga, qb, kc, vc, ks, vs, kw, vw, nsa_g, merge_a, merge_b) = jnp.split(proj, offsets, axis=-1)
    b_, t_, _ = xn.shape

    oa = hgrn2_mixer(qa, fa, ia, ga, lb)
    oa = oa * lax.rsqrt(jnp.mean(oa * oa, axis=-1, keepdims=True) + EPS)
    oa = (oa.reshape(b_, t_, D_A) * a_norm_g.astype(jnp.float32)).astype(xn.dtype) * jax.nn.silu(ga)
    ya = oa @ w_proj_a

    ob = nsa_mixer(qb, kc, vc, ks, vs, kw, vw, nsa_g, pe_k, w1k, b1k, w2k, b2k, pe_v, w1v, b1v, w2v, b2v)
    yb = ob @ w_proj_b

    merged = jax.nn.sigmoid(merge_a) * ya + jax.nn.sigmoid(merge_b) * yb
    return merged @ w_out

def swiglu(h, w_gate, w_up, w_down):
    return (jax.nn.silu(h @ w_gate) * (h @ w_up)) @ w_down

def setup_inputs(seed: int = 0) -> dict:
    key = jax.random.key(seed)
    ks = jax.random.split(key, 32)
    L = DEPTH

    def nrm(k, shape, scale):
        return jax.random.normal(k, shape, jnp.float32) * scale

    def gain(k, shape):
        return 1.0 + 0.1 * jax.random.normal(k, shape, jnp.float32)

    flat = CMP_BLOCK * B_HEAD_DIM
    return {
        "x": nrm(ks[0], (BATCH, SEQ, D_MODEL), 1.0),
        "pre_mix_g": gain(ks[1], (L, D_MODEL)),
        "w_in": nrm(ks[2], (L, D_MODEL, IN_COLS), D_MODEL ** -0.5),
        "lb_table": nrm(ks[3], (L + 1, D_A), 0.5),
        "a_norm_g": gain(ks[4], (L, D_A)),
        "cmp_pe_k": nrm(ks[5], (L, CMP_BLOCK, B_HEAD_DIM), 0.1),
        "cmp_w1_k": nrm(ks[6], (L, flat, CMP_HIDDEN), flat ** -0.5),
        "cmp_b1_k": nrm(ks[7], (L, CMP_HIDDEN), 0.01),
        "cmp_w2_k": nrm(ks[8], (L, CMP_HIDDEN, B_HEAD_DIM), CMP_HIDDEN ** -0.5),
        "cmp_b2_k": nrm(ks[9], (L, B_HEAD_DIM), 0.01),
        "cmp_pe_v": nrm(ks[10], (L, CMP_BLOCK, B_HEAD_DIM), 0.1),
        "cmp_w1_v": nrm(ks[11], (L, flat, CMP_HIDDEN), flat ** -0.5),
        "cmp_b1_v": nrm(ks[12], (L, CMP_HIDDEN), 0.01),
        "cmp_w2_v": nrm(ks[13], (L, CMP_HIDDEN, B_HEAD_DIM), CMP_HIDDEN ** -0.5),
        "cmp_b2_v": nrm(ks[14], (L, B_HEAD_DIM), 0.01),
        "w_proj_a": nrm(ks[15], (L, D_A, D_MODEL), D_A ** -0.5),
        "w_proj_b": nrm(ks[16], (L, D_B, D_MODEL), D_B ** -0.5),
        "w_out": nrm(ks[17], (L, D_MODEL, D_MODEL), D_MODEL ** -0.5),
        "post_mix_g": gain(ks[18], (L, D_MODEL)),
        "pre_ffn_g": gain(ks[19], (L, D_MODEL)),
        "w_gate": nrm(ks[20], (L, D_MODEL, D_FF), D_MODEL ** -0.5),
        "w_up": nrm(ks[21], (L, D_MODEL, D_FF), D_MODEL ** -0.5),
        "w_down": nrm(ks[22], (L, D_FF, D_MODEL), D_FF ** -0.5),
        "post_ffn_g": gain(ks[23], (L, D_MODEL)),
    }

def reference(x, pre_mix_g, w_in, lb_table, a_norm_g, cmp_pe_k, cmp_w1_k, cmp_b1_k, cmp_w2_k, cmp_b2_k,
              cmp_pe_v, cmp_w1_v, cmp_b1_v, cmp_w2_v, cmp_b2_v, w_proj_a, w_proj_b, w_out, post_mix_g,
              pre_ffn_g, w_gate, w_up, w_down, post_ffn_g):
    lb_all = jnp.cumsum(jax.nn.softmax(lb_table.astype(jnp.float32), axis=0), axis=0)
    h = x
    for l in range(DEPTH):
        mix = hybrid_mixer(rms_norm(h, pre_mix_g[l]), w_in[l], lb_all[l], a_norm_g[l],
                           cmp_pe_k[l], cmp_w1_k[l], cmp_b1_k[l], cmp_w2_k[l], cmp_b2_k[l],
                           cmp_pe_v[l], cmp_w1_v[l], cmp_b1_v[l], cmp_w2_v[l], cmp_b2_v[l],
                           w_proj_a[l], w_proj_b[l], w_out[l])
        h = h + rms_norm(mix, post_mix_g[l])
        ff = swiglu(rms_norm(h, pre_ffn_g[l]), w_gate[l], w_up[l], w_down[l])
        h = h + rms_norm(ff, post_ffn_g[l])
    return h


_drawn_inputs = setup_inputs


def setup_inputs(seed=0):
    import zlib

    import numpy as np

    out = dict(_drawn_inputs(seed))
    spreads = {}
    factors = {'cmp_pe_k': 8.0, 'cmp_b1_k': 64.0, 'cmp_b2_k': 200.0, 'cmp_b1_v': 8.0, 'cmp_b2_v': 8.0}
    for name, (base, spread) in spreads.items():
        noise = np.random.default_rng([zlib.crc32(name.encode()), seed]).standard_normal(out[name].shape)
        drawn = base * np.exp(spread * noise) if base else spread * noise
        out[name] = __import__('jax').numpy.asarray(drawn.astype(out[name].dtype))
    for name, factor in factors.items():
        out[name] = (out[name] * factor).astype(out[name].dtype)
    return out
```

```python
from contextlib import ExitStack

import numpy as np
import concourse.bass as bass
from concourse import mybir

F32 = mybir.dt.float32
F32R = mybir.dt.float32r
BF16 = mybir.dt.bfloat16
U32 = mybir.dt.uint32
ALU = mybir.AluOpType
ACT = mybir.ActivationFunctionType
AX = mybir.AxisListType

P = 128
T = 512
D = 2048
DT = D // P
FF = 5632
FT = FF // P
NT = T // P
CH = 256
KU = 4
UN = KU * CH
RING = 4
AHEAD = 3
H_A = 8
H_B = 16
KV = 4
GRP = H_B // KV
DH = 64
NC = 32
CB = 31
LEVELS = 8
EPS = 1e-6
NEG = -1e30

KB = 1024
BASE = 16512
XREG = BASE + 48 * KB
Z = BASE + 112 * KB
TOP = BASE + 204 * KB

A1, A2, B_, C_ = 6, 4, 16, 16
D_, E_ = 8, 8
PARTS = FT // KU
U_A1 = 0
U_A2 = U_A1 + 4 * A1
U_B = U_A2 + 4 * A2
U_C = U_B + 4 * B_
U_D = U_C + 4 * C_
U_E = U_D + 4 * D_
U_G = U_E + 4 * E_
U_G1 = U_G + 16
U_H = U_G1 + 24 * (PARTS - 1)
U_END = U_H + 8
TILE_KC, TILE_VC, TILE_KS, TILE_VS, TILE_KW, TILE_VW, TILE_Q = 0, 2, 4, 6, 8, 10, 12
TILE_HQ, TILE_HF, TILE_HI, TILE_HG, TILE_MA, TILE_MB = 20, 28, 36, 44, 52, 68
V_PRE, V_POST, V_PREF, V_POSTF, V_AN, V_L0, V_L1, V_B1K, V_B1V = 0, 16, 32, 48, 64, 72, 80, 88, 90
V_N = 92
K_ID, K_ROT, K_DIAG, K_CM, K_C01, K_CQ, K_SQ, K_CK, K_SK, K_CC, K_SC = (
    0, 128, 256, 384, 512, 640, 1152, 1664, 2176, 2688, 2720)
K_N = 2752


def hybrid_block(nc, x_t, w_a, w_b, w_c, w_d, w_e, w_g, w_h, w_gate, vecs, consts, level_mask,
                 pe_k, pe_v, w1_k, w1_v, w2_k, w2_v, b2, out):
    with ExitStack() as ctx:
        def at(name, shape, dt, where):
            return nc.alloc_sbuf_tensor_at(name, shape, dt, offset=int(where))

        def sem(name):
            return ctx.enter_context(nc.semaphore(name))

        proj = nc.dram_tensor("proj_scratch", [84, P, T], F32, kind="Internal").ap()
        hscr = nc.dram_tensor("h_scratch", [DT, P, T], F32, kind="Internal").ap()

        raw = [at(f"w_raw{r}", [P, UN], F32, BASE + 4 * KB * r) for r in range(RING)]
        whi = [at(f"w_hi{r}", [P, UN], F32R, BASE + 16 * KB + 4 * KB * r) for r in range(RING)]
        wlo = [at(f"w_lo{r}", [P, UN], F32R, BASE + 32 * KB + 4 * KB * r) for r in range(RING)]
        XH = at("act_hi", [P, DT, T], F32R, XREG)
        XL = at("act_lo", [P, DT, T], F32R, XREG + 32 * KB)
        ident = at("ident", [P, P], F32, TOP)
        ones = at("ones", [P, P], F32, TOP + 512)
        vec = at("vec", [P, V_N], F32, TOP + 1024)
        eps = at("eps", [P, 1], F32, TOP + 1536)
        lb = at("lb", [P, H_A], F32, TOP + 1568)
        olb = at("one_minus_lb", [P, H_A], F32, TOP + 1600)
        pe2 = at("pe2", [P, 2, 16], F32, TOP + 1632)
        w2s = at("w2s", [P, 2, 2, DH], F32, TOP + 1760)
        b2s = at("b2s", [DH, 2], F32, TOP + 2784)
        negmax = at("negmax", [P, 2], F32, TOP + 2816)
        expsum = at("expsum", [P, 2], F32, TOP + 2848)
        rsum = at("rsum", [P, 2], F32, TOP + 2880)
        cstat = at("cstat", [P, 3, 4], F32, TOP + 2912)
        waited = at("waited", [P, LEVELS], F32, TOP + 3616)
        c01 = at("cmp_mask01", [P, 4, NC], F32, TOP + 3072)
        XS = at("x_in", [P, DT, T], F32, Z)
        SQ = at("squares", [P, 2, T], F32, Z + 32 * KB)
        RSTD = at("rstd", [P, T], F32, Z + 36 * KB)
        TN = at("normed", [P, 2, T], F32, Z + 38 * KB)
        cload = at("const_load", [P, 256], F32, Z + 52 * KB)
        lbt = at("lb_tmp", [P, 3, H_A], F32, Z + 54 * KB)
        Kb = at("keys", [P, KV, T], F32, Z)
        Vb = at("values", [P, 2, NT, KV * DH], F32, Z + 8 * KB)
        Qb = at("queries", [P, H_B, T], F32, Z + 16 * KB)
        wgf = at("wg_f", [P, DT, 48], F32, Z + 16 * KB)
        wgh = at("wg_hi", [P, DT, 48], F32R, Z + 19 * KB)
        wgl = at("wg_lo", [P, DT, 48], F32R, Z + 22 * KB)
        kcs = at("rope_k", [P, 2, T], F32, Z + 36 * KB)
        Vst = at("v_stage", [P, 2, 2, T], F32, Z + 40 * KB)
        KD = at("cmp_in", [P, KV, T], F32, Z + 48 * KB)
        Rb = at("cmp_blocks", [P, 16, KV, CB], F32, Z + 56 * KB)
        otok = at("attn_out", [P, NT, H_B * DH], F32, Z + 48 * KB)
        KC = at("k_cmp", [DH, KV, NC], F32, Z + 64 * KB)
        VC = at("v_cmp", [NC, KV, DH], F32, Z + 64 * KB + 512)
        rot = at("rot", [P, P], F32, Z + 65 * KB + 512)
        w1s = at("w1s", [P, 16, CH], F32, Z + 66 * KB)
        ccs = at("rope_cmp", [DH, 2, NC], F32, Z + 82 * KB)
        qcs = at("rope_q", [P, 2, T], F32, Z + 66 * KB)
        QR = at("q_rot", [P, 2, T], F32, Z + 88 * KB)
        Pb = at("probs", [P, 2, T], F32, Z + 72 * KB)
        PT = at("probs_t", [P, 2, T], F32, Z + 76 * KB)
        PC = at("probs_cmp", [P, 4, NC], F32, Z + 80 * KB)
        PCT = at("probs_cmp_t", [NC, T], F32, Z + 80 * KB + 512)
        VG = at("group_values", [P, 2, NT, DH], F32, Z + 70 * KB)
        VCG = at("group_v_cmp", [NC, DH], F32, TOP + 3680)
        maskb = at("diag_mask", [P, P], BF16, Z + 82 * KB + 512)
        cmaskb = at("cmp_mask", [P, P], BF16, Z + 82 * KB + 768)
        gates = at("gates", [P, NT, 48], F32, Z + 83 * KB)
        identb = at("ident_bf", [P, P], BF16, Z + 83 * KB + 768)
        OS = at("out_stage", [P, 2, T], F32, Z + 84 * KB)
        HG = at("cmp_hidden", [P, 2, KV * CB], F32, Z + 34 * KB)
        cmpo = at("cmp_out", [DH, KV, NC], F32, Z + 35 * KB)
        LQ, LF, LI, LG, SIG, LP, LX = [at(n, [P, T], F32, Z + 2 * KB * i) for i, n in enumerate(
            ["in_q", "in_f", "in_i", "in_g", "sig", "prefix", "suffix"])]
        QT = at("q_decayed", [P, 2, T], F32, Z + 14 * KB)
        KT = at("k_decayed", [P, 2, T], F32, Z + 18 * KB)
        EQ = at("decay_q", [P, T // 2], F32, Z + 22 * KB)
        EK = at("decay_k", [P, T // 2], F32, Z + 23 * KB)
        ATT = at("att_t", [P, NT, P], F32, Z + 24 * KB)
        ITOK = at("i_tok", [P, NT, P], F32, Z + 26 * KB)
        KETOK = at("k_tok", [P, 3, P], F32, Z + 28 * KB)
        ST = at("state", [P, 3, P], F32, Z + 30 * KB)
        EB, EX, QE, KE, SG, OSQ, ORS, KF = [at(n, [P, T], F32, Z + 32 * KB + 2 * KB * i) for i, n in enumerate(
            ["decay_all", "decay_rest", "q_all", "k_rest", "silu_g", "o_sq", "o_rstd", "k_f"])]
        lmask = at("level_masks", [P, LEVELS, P], F32, Z + 88 * KB)
        SGM = at("sig_g", [P, T], F32, Z + 65 * KB)
        OAF = at("oa", [P, H_A, T], F32, Z + 67 * KB)
        OBH, OBL, OAH, OAL = [at(n, [P, 8, T], F32R, Z + 16 * KB * i) for i, n in enumerate(
            ["ob_hi", "ob_lo", "oa_hi", "oa_lo"])]
        MG = at("merge_gates", [P, 2, 4, T], F32, Z + 67 * KB)
        MT = at("merge_tmp", [P, 2, T], F32, Z + 83 * KB)
        MS = at("merged", [P, 2, T], F32, Z + 87 * KB)
        MIX = at("mix", [P, DT, T], F32, Z)
        HX = at("residual", [P, DT, T], F32, Z + 32 * KB)
        SQ2 = at("squares2", [P, 2, T], F32, Z + 64 * KB)
        SACC = at("square_sum", [P, T], F32, Z + 68 * KB)
        RS1 = at("rstd1", [P, T], F32, Z + 70 * KB)
        RS2 = at("rstd2", [P, T], F32, Z + 72 * KB)
        TN2 = at("normed2", [P, 2, T], F32, Z + 74 * KB)
        FFA = at("ffn_sum", [P, DT, T], F32, Z)
        HH = at("hidden_hi", [P, 6, T], F32R, Z + 64 * KB)
        HL = at("hidden_lo", [P, 6, T], F32R, Z + 76 * KB)
        GT = at("gated", [P, 2, T], F32, Z + 88 * KB)
        SACC2 = at("square_sum2", [P, T], F32, XREG)
        RS3 = at("rstd3", [P, T], F32, XREG + 2 * KB)
        SQ3 = at("squares3", [P, 2, T], F32, XREG + 4 * KB)

        ps = ctx.enter_context(nc.psum_tensor("ps", [P, 8, T], F32))

        landed = [sem(f"unit_landed{r}") for r in range(RING)]
        hi_ready, lo_ready, unit_done = sem("hi_ready"), sem("lo_ready"), sem("unit_done")
        x_in = [sem(f"x_in{i}") for i in range(4)]
        vec_in, consts_in, ones_ok, consts_ok = sem("vec_in"), sem("consts_in"), sem("ones_ok"), sem("consts_ok")
        sq_ready, sq_used, mean_ready, std_ready, rstd_ready = (sem(n) for n in (
            "sq_ready", "sq_used", "mean_ready", "std_ready", "rstd_ready"))
        tn_ready, act_hi, act_lo = sem("tn_ready"), sem("act_hi"), sem("act_lo")
        proj_taken = sem("proj_taken")
        stored = sem("proj_stored")
        kraw_in, kcs_in, vst_in, w1_in, kd_in, q_in, qcs_in = (sem(n) for n in (
            "kraw_in", "kcs_in", "vst_in", "w1_in", "kd_in", "q_in", "qcs_in"))
        krot_done, k_ready, vt_done, v_ready, vg_ready = (sem(n) for n in (
            "krot_done", "k_ready", "vt_done", "v_ready", "vg_ready"))
        blocks_ready, hid_done, gelu_done, cmp_done, cmp_biased, crot_done, kc_ready, vct_done, vc_ready = (
            sem(n) for n in ("blocks_ready", "hid_done", "gelu_done", "cmp_done", "cmp_biased", "crot_done",
                             "kc_ready", "vct_done", "vc_ready"))
        wg_in, wg_hi_ok, wg_lo_ok, glog_done, gates_ready = (sem(n) for n in (
            "wg_in", "wg_hi_ok", "wg_lo_ok", "glog_done", "gates_ready"))
        qrot_done, q_ready, s_done, max_ready, exp_done, p_ready, t_done, pt_ready, v_done, o_ready = (
            sem(n) for n in ("qrot_done", "q_ready", "s_done", "max_ready", "exp_done", "p_ready", "t_done",
                             "pt_ready", "v_done", "o_ready"))
        lm_in, q_ld, f_ld, i_ld, g_ld = (sem(n) for n in ("lm_in", "q_ld", "f_ld", "i_ld", "g_ld"))
        sig_done, f_ready, ln_done, sgm_done, sg_ready, itr_done, itok_ready = (sem(n) for n in (
            "sig_done", "f_ready", "ln_done", "sgm_done", "sg_ready", "itr_done", "itok_ready"))
        dec_done, qk_ready, px_ready, lev_done, att_taken = (sem(n) for n in (
            "dec_done", "qk_ready", "px_ready", "lev_done", "att_taken"))
        fin_exp, fin_ready, ktr_done, ktok_ready, g_done, st_ready, ro_done, osq_ready, omean_done, ostd_ready, oa_ready = (
            sem(n) for n in ("fin_exp", "fin_ready", "ktr_done", "ktok_ready", "g_done", "st_ready", "ro_done",
                             "osq_ready", "omean_done", "ostd_ready", "oa_ready"))
        ot_done, mg_ready = sem("ot_done"), sem("mg_ready")
        mg_in = [sem(f"mg_in{i}") for i in range(2)]
        blk_taken, ms_ready = sem("blk_taken"), sem("ms_ready")
        pair_sq, ssum_ready, hx_in, h_ready, hsq_ready = (sem(n) for n in (
            "pair_sq", "ssum_ready", "hx_in", "h_ready", "hsq_ready"))
        silu_ready, hid_hi, hid_lo, out_ready, out_done = (sem(n) for n in (
            "silu_ready", "hid_hi", "hid_lo", "out_ready", "out_done"))
        lb_shifted, lb_exp = sem("lb_shifted"), sem("lb_exp")

        block = ctx.enter_context(nc.Block())

        def col(v, k):
            return vec[:, v + k:v + k + 1]

        def halves(t, w):
            v = t[:].rearrange("p (b h w) -> p b h w", h=2, w=w)
            return v[:, :, 0, :], v[:, :, 1, :]

        def flat(t, w):
            return t[:].rearrange("p (b w) -> p b w", w=w)

        @block.sync
        def _(sp):
            for g in range(4):
                sp.dma_start(XS[:, 4 * g:4 * g + 4, :],
                             x_t[4 * g:4 * g + 4].rearrange("k p t -> p k t")).then_inc(x_in[g], 16)

            def load(u0, per, i, s, src, wait=True):
                u = u0 + per * i + s
                if wait:
                    sp.wait_ge(lo_ready, u - RING + 1)
                sp.dma_start(raw[(u0 + s) % RING][:], src).then_inc(landed[(u0 + s) % RING], 16)

            def cut(w, c, k):
                return w[c][:, k * UN:(k + 1) * UN]

            for s in range(8):
                load(0, 0, 0, s, cut(w_a, s // 4, s % 4), wait=s >= RING)
            with sp.Fori(1, A1 // 2) as i:
                for s in range(8):
                    load(U_A1, 8, i, s, cut(w_a, 2 * i + s // 4, s % 4))
            for s in range(4 * A2):
                load(U_A2, 0, 0, s, cut(w_a, A1 + s // 4, s % 4))
            for u0, w, n in ((U_B, w_b, B_), (U_C, w_c, C_), (U_D, w_d, D_), (U_E, w_e, E_)):
                with sp.Fori(0, n // 2) as i:
                    for s in range(8):
                        load(u0, 8, i, s, cut(w, 2 * i + s // 4, s % 4))
            for s in range(16):
                load(U_G, 0, 0, s, cut(w_g, s // 8, s % 8))
            with sp.Fori(0, (PARTS - 1) // 2) as i:
                for half in range(2):
                    for s in range(8):
                        load(U_G1, 48, i, 24 * half + s, cut(w_g, 4 * i + 2 * half + 2, s))
                    for s in range(8):
                        load(U_G1, 48, i, 24 * half + 8 + s, cut(w_h, 2 * i + half, s))
                    for s in range(8):
                        load(U_G1, 48, i, 24 * half + 16 + s, cut(w_g, 4 * i + 2 * half + 3, s))
            for s in range(8):
                load(U_H, 0, 0, s, cut(w_h, PARTS - 1, s))
            for k in range(0, DT, 4):
                sp.wait_ge(out_ready, k + 4)
                sp.dma_start(out[k:k + 4].rearrange("k p t -> p k t"), FFA[:, k:k + 4, :]).then_inc(out_done, 16)
            sp.wait_ge(out_done, 16 * (DT // 4))

        @block.gpsimd
        def _(pool):
            for s in (exp_done, pt_ready, v_done, t_done, o_ready, unit_done, att_taken, oa_ready, ms_ready, hid_lo,
                      proj_taken, proj_taken, blk_taken, blk_taken):
                pool.sem_inc(s, 1)
            pool.dma_start(vec[:], vecs).then_inc(vec_in, 16)
            pool.dma_start(cload[:, 0:256], consts[:, K_DIAG:K_DIAG + 256]).then_inc(consts_in, 16)
            pool.dma_start(ident[:], consts[:, K_ID:K_ID + P]).then_inc(consts_in, 16)
            pool.dma_start(rot[:], consts[:, K_ROT:K_ROT + P]).then_inc(consts_in, 16)
            pool.dma_start(c01[:].rearrange("p a b -> p (a b)"), consts[:, K_C01:K_C01 + P]).then_inc(consts_in, 16)
            pool.dma_start(pe2[:, 0, :], pe_k).then_inc(consts_in, 16)
            pool.dma_start(pe2[:, 1, :], pe_v).then_inc(consts_in, 16)
            pool.dma_start(w2s[:, 0], w2_k).then_inc(consts_in, 16)
            pool.dma_start(w2s[:, 1], w2_v).then_inc(consts_in, 16)
            pool.dma_start(b2s[:], b2).then_inc(consts_in, 16)
            pool.wait_ge(act_lo, DT)
            pool.dma_start(wgf[:], w_gate).then_inc(wg_in, 16)
            pool.dma_start(kcs[:], consts[:, K_CK:K_CK + 2 * T].rearrange("p (a t) -> p a t", a=2)).then_inc(kcs_in, 16)
            pool.dma_start(ccs[:], consts[0:DH, K_CC:K_CC + 2 * NC].rearrange("p (a t) -> p a t", a=2)).then_inc(kcs_in, 16)
            pool.dma_start(w1s[:], w1_k).then_inc(w1_in, 16)

            def store(n):
                pool.wait_ge(proj_taken, 2 + n + 1)
                pool.dma_start(proj[bass.ds(2 * n, 2)].rearrange("m p t -> p m t"), OS[:]).then_inc(stored, 16)

            def spread(dst, tile, rows, halves_to, semaphore, shift=0):
                for half in range(2):
                    src = proj[tile:tile + 2, 64 * half:64 * half + 64, :].rearrange("m p t -> p m t")
                    pool.dma_start(dst[halves_to:halves_to + DH, half::2, 0:T - shift],
                                   src[:, :, shift:T]).then_inc(semaphore, 16)

            with pool.Fori(0, A1 // 2) as i:
                for par in range(2):
                    store(2 * i + par)
            pool.wait_ge(stored, 16 * A1)
            spread(Kb, TILE_KS, DH, 0, kraw_in)
            spread(Kb, TILE_KW, DH, DH, kraw_in)
            for b, tile in enumerate((TILE_VS, TILE_VW)):
                pool.dma_start(Vst[:, b], proj[tile:tile + 2].rearrange("m p t -> p m t")).then_inc(vst_in, 16)
            spread(KD, TILE_KC, DH, 0, kd_in)
            spread(KD, TILE_KC, DH, DH, kd_in, shift=1)
            store(A1)
            store(A1 + 1)
            pool.wait_ge(hid_done, 1)
            pool.dma_start(w1s[:], w1_v).then_inc(w1_in, 16)
            spread(KD, TILE_VC, DH, 0, kd_in)
            spread(KD, TILE_VC, DH, DH, kd_in, shift=1)

            def queries(c):
                pool.wait_ge(stored, 16 * (A1 + c + 1))
                for dup in range(2):
                    for half in range(2):
                        src = proj[TILE_Q + 2 * c:TILE_Q + 2 * c + 2, 64 * half:64 * half + 64, :]
                        pool.dma_start(Qb[DH * dup:DH * dup + DH, 4 * c + half:4 * c + half + 3:2, :],
                                       src.rearrange("m p t -> p m t")).then_inc(q_in, 16)
                pool.wait_ge(q_in, 64 * (c + 1))

            pool.wait_ge(glog_done, 1)
            queries(0)
            queries(1)
            store(A1 + 2)
            pool.wait_ge(hid_done, 2)
            pool.dma_start(qcs[:], consts[:, K_CQ:K_CQ + 2 * T].rearrange("p (a t) -> p a t", a=2)).then_inc(qcs_in, 16)
            pool.wait_ge(v_ready, 4)
            pool.wait_ge(vc_ready, 1)
            pool.wait_ge(kc_ready, 1)
            queries(2)
            store(A1 + 3)
            queries(3)
            with pool.Fori(0, KV) as kv:
                pool.wait_ge(v_done, 1 + 32 * kv)
                pool.tensor_copy(VG[:], Vb[:, :, :, bass.ds(kv * DH, DH)])
                pool.tensor_copy(VCG[:], VC[:, kv, :]).then_inc(vg_ready, 1)
                for g in range(GRP):
                    store(A1 + A2 + GRP * kv + g)

            pool.wait_ge(stored, 16 * (A1 + A2 + B_))
            pool.wait_ge(o_ready, 1 + H_B)
            pool.dma_start(lmask[:].rearrange("p l t -> p (l t)"), level_mask).then_inc(lm_in, 16)

            def fetch(h):
                pool.dma_start(LF[:], proj[TILE_HF + h]).then_inc(f_ld, 16)
                pool.dma_start(LG[:], proj[TILE_HG + h]).then_inc(g_ld, 16)
                pool.dma_start(LI[:], proj[TILE_HI + h]).then_inc(i_ld, 16)
                pool.dma_start(LQ[:], proj[TILE_HQ + h]).then_inc(q_ld, 16)

            fetch(0)
            n_c = A1 + A2 + B_
            with pool.Fori(0, H_A - 1) as h:
                store(n_c + 2 * h)
                pool.wait_ge(fin_ready, h + 1)
                pool.wait_ge(sg_ready, h + 1)
                pool.wait_ge(itr_done, h + 1)
                fetch(h + 1)
                store(n_c + 2 * h + 1)
            store(n_c + 2 * H_A - 2)
            store(n_c + 2 * H_A - 1)
            pool.wait_ge(stored, 16 * (n_c + 2 * H_A))
            pool.wait_ge(act_lo, DT + 16)

            def merge_gates(c, par):
                pool.dma_start(MG[:, par, 0:2, :], proj[bass.ds(TILE_MA + 2 * c, 2)].rearrange("m p t -> p m t")).then_inc(mg_in[par], 16)
                pool.dma_start(MG[:, par, 2:4, :], proj[bass.ds(TILE_MB + 2 * c, 2)].rearrange("m p t -> p m t")).then_inc(mg_in[par], 16)

            merge_gates(0, 0)
            with pool.Fori(0, D_ // 2 - 1) as i:
                pool.wait_ge(ms_ready, 1 + 2 * i)
                merge_gates(2 * i + 1, 1)
                pool.wait_ge(ms_ready, 1 + 2 * i + 1)
                merge_gates(2 * i + 2, 0)
            pool.wait_ge(ms_ready, 1 + D_ - 2)
            merge_gates(D_ - 1, 1)
            pool.wait_ge(unit_done, 1 + U_E)
            for g in range(4):
                pool.dma_start(HX[:, 4 * g:4 * g + 4, :],
                               x_t[4 * g:4 * g + 4].rearrange("k p t -> p k t")).then_inc(hx_in, 16)

        def split_hi(act, u0, per, i, s):
            s = s + AHEAD
            u = u0 + per * i + s
            r = (u0 + s) % RING
            if u0 + s >= RING:
                act.wait_ge(unit_done, 1 + u - RING + 1)
            act.wait_ge(landed[r], 16 * ((u0 + s) // RING + (per // RING) * i + 1))
            nc.scalar.activation(whi[r][:], raw[r][:], ACT.Copy).then_inc(hi_ready, 1)

        def split_lo(dve, u0, per, i, s):
            s = s + AHEAD
            r = (u0 + s) % RING
            dve.wait_ge(hi_ready, u0 + per * i + s + 1)
            nc.vector.tensor_tensor(wlo[r][:], raw[r][:], whi[r][:].bitcast(F32), ALU.subtract).then_inc(lo_ready, 1)

        @block.tensor
        def _(pe):
            def mm(o, l, r, start, stop):
                return nc.tensor.matmul(o, l, r, start=start, stop=stop, skip_group_check=True)

            def unit(u0, per, i, s, hi, lo, k0, bank, first, last, side=None, split=None):
                if split is not None:
                    pe.wait_ge(act_lo, split)
                u = u0 + per * i + s
                r = (u0 + s) % RING
                pe.wait_ge(lo_ready, u + 1)
                for j in range(KU):
                    for m in range(2):
                        w = slice(j * CH + m * P, j * CH + m * P + P)
                        o = ps[:, bank + m, :]
                        mm(o, whi[r][:, w], hi[:, k0 + j, :], first and j == 0, False)
                        mm(o, whi[r][:, w], lo[:, k0 + j, :], False, False)
                        done = mm(o, wlo[r][:, w], hi[:, k0 + j, :], False, last and j == KU - 1)
                    if j == KU - 1:
                        done.then_inc(unit_done, 1)
                    if side is not None:
                        side(4 * s + j)
                return done

            def proj_chunk(u0, per, i, s0, n, side=None, split=False):
                par = (s0 // 4) % 2
                pe.wait_ge(proj_taken, 1 + n)
                for q in range(4):
                    last = unit(u0, per, i, s0 + q, XH, XL, 4 * q, 2 * par, q == 0, q == 3,
                                side, 4 * q + 4 if split else None)
                return last

            for k in range(DT):
                pe.wait_ge(sq_ready, k + 1)
                if k == 0:
                    pe.wait_ge(ones_ok, 1)
                mm(ps[:, 7, :], ones[:], SQ[:, k % 2, :], k == 0, k == DT - 1).then_inc(sq_used, 1)

            with pe.Fori(0, A1 // 2) as i:
                for par in range(2):
                    proj_chunk(U_A1, 8, i, 4 * par, 2 * i + par, split=(par == 0))

            def prepare(t):
                if t in (8, 10, 12, 14):
                    kv = (t - 8) // 2
                    if kv == 0:
                        pe.wait_ge(kraw_in, 64)
                        pe.wait_ge(consts_ok, 1)
                    if kv >= 2:
                        pe.wait_ge(k_ready, kv - 1)
                    mm(ps[:, 4 + kv % 2, :], rot[:], Kb[:, kv, :], True, True).then_inc(krot_done, 1)
                if t in (16, 18, 20, 22):
                    g = (t - 16) // 2
                    b, m = g // 2, g % 2
                    if g == 0:
                        pe.wait_ge(vst_in, 32)
                        pe.wait_ge(gates_ready, 1)
                    if g >= 2:
                        pe.wait_ge(v_ready, g - 1)
                    for kb in range(NT):
                        o = nc.tensor.transpose(ps[:, 6 + g % 2, kb * P:kb * P + P], Vst[:, b, m, kb * P:kb * P + P], ident[:])
                    o.then_inc(vt_done, 1)
                for x, t0 in ((0, 24), (1, 42)):
                    if t0 <= t < t0 + 8:
                        if t == t0:
                            pe.wait_ge(blocks_ready, x + 1)
                            pe.wait_ge(w1_in, 16 * (x + 1))
                            pe.wait_ge(k_ready, KV)
                            pe.wait_ge(gelu_done, x)
                        for jm in range(4 * (t - t0), 4 * (t - t0) + 4):
                            m, j = jm // 16, jm % 16
                            o = mm(ps[:, 4, m * 128:m * 128 + KV * CB], w1s[:, j, m * P:m * P + P],
                                   Rb[:, j].rearrange("p a b -> p (a b)"), j == 0, j == 15)
                        if t == t0 + 7:
                            o.then_inc(hid_done, 1)
                    if t == t0 + 9:
                        pe.wait_ge(gelu_done, x + 1)
                        for m in range(2):
                            o = mm(ps[0:DH, 5, 0:KV * CB], w2s[:, x, m, :], HG[:, m, :], m == 0, m == 1)
                        o.then_inc(cmp_done, 1)
                if t == 36:
                    pe.wait_ge(cmp_biased, 1)
                    pe.wait_ge(v_ready, 4)
                    mm(ps[0:DH, 6, 0:KV * NC], rot[0:DH, 0:DH], cmpo[:].rearrange("p a b -> p (a b)"), True, True).then_inc(crot_done, 1)
                if t == 54:
                    pe.wait_ge(cmp_biased, 2)
                    for kv in range(KV):
                        o = nc.tensor.transpose(ps[0:NC, 7, kv * DH:kv * DH + DH], cmpo[:, kv, :], ident[0:DH, 0:DH])
                    o.then_inc(vct_done, 1)
                if t < NT:
                    if t == 0:
                        pe.wait_ge(wg_lo_ok, 1)
                    for k in range(DT):
                        for a, (l, r) in enumerate(((XH, wgh), (XL, wgh), (XH, wgl))):
                            o = mm(ps[:, 6, t * 48:t * 48 + 48], l[:, k, t * P:t * P + P], r[:, k, :],
                                   k == 0 and a == 0, k == DT - 1 and a == 2)
                    if t == NT - 1:
                        o.then_inc(glog_done, 1)

            for c in range(A2):
                proj_chunk(U_A2, 0, 0, 4 * c, A1 + c, prepare)

            pe.wait_ge(q_ready, 1)
            with pe.Fori(0, KV) as kv:
                pe.wait_ge(q_in, 64 * (kv + 1))
                for g in range(GRP):
                    hd = GRP * kv + g

                    def head(t, hd=hd, kv=kv, g=g):
                        t -= 16 * g
                        if t == 0:
                            pe.wait_ge(exp_done, 1 + 9 * hd)
                            mm(ps[:, 4, :], rot[:], Qb[:, hd, :], True, True).then_inc(qrot_done, 1)
                        k = t - 3
                        if k == 0:
                            pe.wait_ge(kc_ready, 1)
                            pe.wait_ge(q_ready, hd + 2)
                            for tt in range(NT):
                                mm(ps[:, 4, tt * NC:tt * NC + NC], identb[:], cmaskb[:, tt * NC:tt * NC + NC], True, False)
                                o = mm(ps[:, 4, tt * NC:tt * NC + NC], QR[0:DH, 0, tt * P:tt * P + P], KC[:, kv, :], False, True)
                            o.then_inc(s_done, 1)
                        if 1 <= k <= 8:
                            b, tt = (k - 1) % 2, (k - 1) // 2
                            n = P * (tt + 1)
                            if k >= 2:
                                pe.wait_ge(exp_done, 1 + 9 * hd + k - 1)
                            bank = ps[:, 4 + k % 2, :]
                            mm(bank[:, 0:n], QR[:, b, tt * P:tt * P + P], Kb[:, kv, 0:n], True, False)
                            mm(bank[:, n - P:n], identb[:], maskb[:], False, True).then_inc(s_done, 1)
                        k = t - 5
                        if 0 <= k <= 8:
                            pe.wait_ge(p_ready, 9 * hd + k + 1)
                            pe.wait_ge(pt_ready, 1 + 9 * hd + k)
                            if k == 0:
                                for tt in range(NT):
                                    o = nc.tensor.transpose(ps[0:NC, 6, tt * P:tt * P + P], PC[:, tt, :], ident[:])
                            else:
                                for kb in range((k - 1) // 2 + 1):
                                    o = nc.tensor.transpose(ps[:, 6, kb * P:kb * P + P], Pb[:, k % 2, kb * P:kb * P + P], ident[:])
                            o.then_inc(t_done, 1)
                        k = t - 7
                        if 1 <= k <= 8:
                            b, tt = (k - 1) % 2, (k - 1) // 2
                            pe.wait_ge(pt_ready, 1 + 9 * hd + k + 1)
                            if k == 1 and g == 0:
                                pe.wait_ge(vg_ready, kv + 1)
                            if k == 1:
                                pe.wait_ge(o_ready, 1 + hd)
                            o = ps[:, 7, tt * DH:tt * DH + DH]
                            if b == 0:
                                mm(o, PCT[:, tt * P:tt * P + P], VCG[:], True, False)
                            for kb in range(tt + 1):
                                last = mm(o, PT[:, k % 2, kb * P:kb * P + P], VG[:, b, kb, :],
                                          False, b == 1 and kb == tt)
                            last.then_inc(v_done, 1)

                    proj_chunk(U_B, 16, kv, 4 * g, A1 + A2 + hd, head)

            n_c = A1 + A2 + B_
            pe.wait_ge(o_ready, 1 + H_B)
            with pe.Fori(0, H_A) as h:
                def recur(t, h=h):
                    if t == 2:
                        pe.wait_ge(i_ld, 16 * (h + 1))
                        pe.wait_ge(oa_ready, 1 + h)
                        for c in range(NT):
                            o = nc.tensor.transpose(ps[:, 7, c * P:c * P + P], LI[:, c * P:c * P + P], ident[:])
                        o.then_inc(itr_done, 1)
                    lev = (t - 4) // 3
                    if t == 4 + 3 * lev and 0 <= lev < LEVELS:
                        if lev == 0:
                            pe.wait_ge(q_ld, 16 * (h + 1))
                            pe.wait_ge(f_ready, h + 1)
                        else:
                            pe.wait_ge(qk_ready, 7 * h + lev)
                        if lev < 2:
                            pe.wait_ge(att_taken, 1 + 8 * h)
                        else:
                            pe.wait_ge(att_taken, 1 + 8 * h + lev - 1)
                        for c in range(NT):
                            cs = slice(c * P, c * P + P)
                            kk = KF[:, cs] if lev == 0 else KT[:, lev % 2, cs]
                            qq = LQ[:, cs] if lev == 0 else QT[:, lev % 2, cs]
                            o = mm(ps[:, 4 + lev % 2, cs], kk, qq, True, True)
                        o.then_inc(lev_done, 1)
                    if t == 26:
                        pe.wait_ge(fin_ready, h + 1)
                        for c in range(NT - 1):
                            o = nc.tensor.transpose(ps[:, 6, c * P:c * P + P], KE[:, c * P:c * P + P], ident[:])
                        o.then_inc(ktr_done, 1)
                    if t == 28:
                        pe.wait_ge(ktok_ready, h + 1)
                        pe.wait_ge(itok_ready, h + 1)
                        for c in range(NT - 1):
                            o = mm(ps[:, 7, c * P:c * P + P], KETOK[:, c, :], ITOK[:, c, :], True, True)
                        o.then_inc(g_done, 1)
                    if t == 30:
                        pe.wait_ge(st_ready, h + 1)
                        pe.wait_ge(att_taken, 1 + 8 * h + 8)
                        for c in range(NT):
                            o = ps[:, 6, c * P:c * P + P]
                            if c:
                                mm(o, ST[:, c - 1, :], QE[:, c * P:c * P + P], True, False)
                            last = mm(o, ITOK[:, c, :], ATT[:, c, :], c == 0, True)
                        last.then_inc(ro_done, 1)
                    if t == 31:
                        pe.wait_ge(osq_ready, h + 1)
                        mm(ps[:, 7, :], ones[:], OSQ[:], True, True).then_inc(omean_done, 1)

                for par in range(2):
                    proj_chunk(U_C, 8, h, 4 * par, n_c + 2 * h + par, recur)

            pe.wait_ge(proj_taken, 2 + n_c + C_)
            pe.wait_ge(oa_ready, 1 + H_A)
            for f in range(8):
                for tt in range(NT):
                    o = nc.tensor.transpose(ps[:, f, tt * P:tt * P + P], otok[:, tt, f * P:f * P + P], ident[:])
                o.then_inc(ot_done, 1)

            pe.wait_ge(act_lo, DT + 16)
            with pe.Fori(0, D_ // 2) as i:
                for half in range(2):
                    pe.wait_ge(blk_taken, 1 + 2 * i + half)
                    for q in range(4):
                        hi, lo = (OAH, OAL) if q < 2 else (OBH, OBL)
                        last = unit(U_D, 8, i, 4 * half + q, hi, lo, 4 * (q % 2), 4 * half + 2 * (q // 2), q % 2 == 0, q % 2 == 1)
            pe.wait_ge(act_lo, DT + 32)
            with pe.Fori(0, E_ // 2) as i:
                for half in range(2):
                    pe.wait_ge(blk_taken, 1 + D_ + 2 * i + half)
                    for q in range(4):
                        unit(U_E, 8, i, 4 * half + q, XH, XL, 4 * q, 4 * half, q == 0, q == 3)
            pe.wait_ge(ssum_ready, E_)
            mm(ps[:, 6, :], ones[:], SACC[:], True, True).then_inc(mean_ready, 1)
            for k in range(DT):
                pe.wait_ge(hsq_ready, k + 1)
                mm(ps[:, 7, :], ones[:], SQ2[:, k % 2, :], k == 0, k == DT - 1).then_inc(sq_used, 1)
            j0 = D_ + E_

            def gate_up(u0, per, i, s0, half, job, split=False):
                pe.wait_ge(blk_taken, 1 + job)
                for q in range(8):
                    unit(u0, per, i, s0 + q, XH, XL, 4 * (q % 4), 4 * half + 2 * (q // 4), q % 4 == 0, q % 4 == 3,
                         split=DT + 32 + 4 * q + 4 if split and q < 4 else None)

            def down(u0, per, i, s0, half, job, parity, tiles):
                pe.wait_ge(hid_lo, 1 + tiles)
                for c in range(8):
                    pe.wait_ge(blk_taken, 1 + job + c)
                    r = (u0 + s0 + c) % RING
                    pe.wait_ge(lo_ready, u0 + per * i + s0 + c + 1)
                    for j in range(KU):
                        place = 2 * parity + j if j < 2 else 2 + j
                        for m in range(2):
                            w = slice(j * CH + m * P, j * CH + m * P + P)
                            o = ps[:, 4 * half + 2 * (c % 2) + m, :]
                            mm(o, whi[r][:, w], HH[:, place, :], j == 0, False)
                            mm(o, whi[r][:, w], HL[:, place, :], False, False)
                            last = mm(o, wlo[r][:, w], HH[:, place, :], False, j == KU - 1)
                    last.then_inc(unit_done, 1)

            gate_up(U_G, 0, 0, 0, 0, j0, split=True)
            gate_up(U_G, 0, 0, 8, 1, j0 + 1)
            with pe.Fori(0, (PARTS - 1) // 2) as i:
                for half in range(2):
                    job = j0 + 2 + 20 * i + 10 * half
                    gate_up(U_G1, 48, i, 24 * half, half, job)
                    down(U_G1, 48, i, 24 * half + 8, 1 - half, job + 1, half, 4 * (2 * i + half) + 4)
                    gate_up(U_G1, 48, i, 24 * half + 16, half, job + 9)
            down(U_H, 0, 0, 0, 0, j0 + 2 + 10 * (PARTS - 1), 0, FT)
            pe.wait_ge(ssum_ready, E_ + 8)
            mm(ps[:, 6, :], ones[:], SACC2[:], True, True).then_inc(mean_ready, 1)

        @block.scalar
        def _(act):
            act_fn = nc.scalar.activation

            def take(u_end, par, n):
                act.wait_ge(unit_done, 1 + u_end)
                if not (isinstance(n, int) and n == 0):
                    act.wait_ge(stored, 16 * n)
                act_fn(OS[:], ps[:, 2 * par:2 * par + 2, :], ACT.Copy).then_inc(proj_taken, 1)

            for k in range(DT):
                act.wait_ge(x_in[k // 4], 16)
                if k >= 2:
                    act.wait_ge(sq_used, k - 1)
                act_fn(SQ[:, k % 2, :], XS[:, k, :], ACT.Square).then_inc(sq_ready, 1)
            for s in range(-AHEAD, 0):
                split_hi(act, 0, 0, 0, s)
            act.wait_ge(sq_used, DT)
            act.wait_ge(ones_ok, 2)
            act_fn(RSTD[:], ps[:, 7, :], ACT.Sqrt, bias=eps[:, 0:1], scale=1.0 / D).then_inc(std_ready, 1)

            def halves_of(tn, base):
                for k in range(DT):
                    act.wait_ge(tn_ready, base + k + 1)
                    act_fn(XH[:, k, :], tn[:, k % 2, :], ACT.Copy).then_inc(act_hi, 1)

            halves_of(TN, 0)
            act.wait_ge(lb_shifted, 1)
            act_fn(lbt[:, 0:2, :], lbt[:, 0:2, :], ACT.Exp).then_inc(lb_exp, 1)

            act.wait_ge(wg_in, 16)
            act_fn(wgh[:], wgf[:], ACT.Copy).then_inc(wg_hi_ok, 1)

            def two_chunks(i):
                for s in range(8):
                    split_hi(act, U_A1, 8, i, s)
                    if s % 4 == 3:
                        take(U_A1 + 8 * i + s + 1, s // 4, 2 * i + s // 4)

            two_chunks(0)
            with act.Fori(1, A1 // 2) as i:
                two_chunks(i)
            for s in range(4 * A2):
                split_hi(act, U_A2, 0, 0, s)
                if s == 1:
                    act.wait_ge(glog_done, 1)
                    act_fn(gates[:].rearrange("p a b -> p (a b)"), ps[:, 6, 0:NT * 48], ACT.Sigmoid).then_inc(gates_ready, 1)
                if s in (4, 5):
                    for g in (2 * (s - 4), 2 * (s - 4) + 1):
                        act.wait_ge(vt_done, g + 1)
                        act_fn(Vb[:, g // 2, :, (g % 2) * P:(g % 2) * P + P],
                               ps[:, 6 + g % 2, :].rearrange("p (a b) -> p a b", a=NT), ACT.Copy).then_inc(v_ready, 1)
                if s in (8, 12):
                    x = (s - 8) // 4
                    act.wait_ge(hid_done, x + 1)
                    for m in range(2):
                        o = act_fn(HG[:, m, :], ps[:, 4, m * 128:m * 128 + KV * CB], ACT.Gelu_apprx_tanh,
                                   bias=col((V_B1K, V_B1V)[x], m))
                    o.then_inc(gelu_done, 1)
                    act.wait_ge(cmp_done, x + 1)
                    if x:
                        act.wait_ge(kc_ready, 1)
                    act_fn(cmpo[:, :, 0:CB], ps[0:DH, 5, 0:KV * CB].rearrange("p (a b) -> p a b", a=KV),
                           ACT.Identity, bias=b2s[:, x:x + 1]).then_inc(cmp_biased, 1)
                if s == 13:
                    act.wait_ge(vct_done, 1)
                    act_fn(VC[:].rearrange("p a b -> p (a b)"), ps[0:NC, 7, 0:KV * DH], ACT.Copy).then_inc(vc_ready, 1)
                if s % 4 == 3:
                    take(U_A2 + s + 1, (s // 4) % 2, A1 + s // 4)

            with act.Fori(0, KV) as kv:
                for g in range(GRP):
                    hd = GRP * kv + g

                    def exps(k):
                        act.wait_ge(max_ready, 9 * hd + k + 1)
                        if k == 0:
                            act_fn(PC[:], PC[:], ACT.Exp).then_inc(exp_done, 1)
                            return
                        act.wait_ge(t_done, 1 + 9 * hd + max(k - 1, 0))
                        n = P * ((k - 1) // 2 + 1)
                        act_fn(Pb[:, k % 2, 0:n], ps[:, 4 + k % 2, 0:n], ACT.Exp, bias=negmax[:, k % 2:k % 2 + 1],
                               accum_out=expsum[:, k % 2:k % 2 + 1]).then_inc(exp_done, 1)

                    def turned(k):
                        act.wait_ge(t_done, 1 + 9 * hd + k + 1)
                        act.wait_ge(v_done, 1 + 8 * hd + max(k - 2, 0))
                        if k == 0:
                            act_fn(PCT[:], ps[0:NC, 6, :], ACT.Copy).then_inc(pt_ready, 1)
                            return
                        n = P * ((k - 1) // 2 + 1)
                        act_fn(PT[:, k % 2, 0:n], ps[:, 6, 0:n], ACT.Copy).then_inc(pt_ready, 1)

                    split_hi(act, U_B, 16, kv, 4 * g)
                    exps(0)
                    split_hi(act, U_B, 16, kv, 4 * g + 1)
                    exps(1)
                    for k in (2, 3, 4):
                        exps(k)
                        turned(k - 2)
                    split_hi(act, U_B, 16, kv, 4 * g + 2)
                    for k in (5, 6, 7, 8):
                        exps(k)
                        turned(k - 2)
                    split_hi(act, U_B, 16, kv, 4 * g + 3)
                    turned(7)
                    turned(8)
                    take(U_B + 16 * kv + 4 * g + 4, g % 2, A1 + A2 + hd)

            with act.Fori(0, H_A) as h:
                def decays(lev):
                    w = 1 << (lev - 1)
                    act.wait_ge(px_ready, 8 * h + lev)
                    if lev == 1:
                        act.wait_ge(ln_done, h + 1)
                    act_fn(flat(EQ, w), halves(LP, w)[1], ACT.Exp)
                    act_fn(flat(EK, w), halves(LX, w)[0], ACT.Exp).then_inc(dec_done, 1)

                split_hi(act, U_C, 8, h, 0)
                act.wait_ge(f_ld, 16 * (h + 1))
                act.wait_ge(oa_ready, 1 + h)
                act_fn(SIG[:], LF[:], ACT.Sigmoid).then_inc(sig_done, 1)
                act.wait_ge(g_ld, 16 * (h + 1))
                act_fn(SGM[:], LG[:], ACT.Sigmoid).then_inc(sgm_done, 1)
                act.wait_ge(f_ready, h + 1)
                act_fn(LP[:], SIG[:], ACT.Ln).then_inc(ln_done, 1)
                act.wait_ge(itr_done, h + 1)
                act_fn(ITOK[:].rearrange("p a b -> p (a b)"), ps[:, 7, :], ACT.Copy).then_inc(itok_ready, 1)
                decays(1)
                split_hi(act, U_C, 8, h, 1)
                decays(2)
                split_hi(act, U_C, 8, h, 2)
                decays(3)
                decays(4)
                split_hi(act, U_C, 8, h, 3)
                decays(5)
                take(U_C + 8 * h + 4, 0, A1 + A2 + B_ + 2 * h)
                split_hi(act, U_C, 8, h, 4)
                decays(6)
                split_hi(act, U_C, 8, h, 5)
                decays(7)
                act.wait_ge(px_ready, 8 * h + 8)
                act_fn(EB[:], LP[:], ACT.Exp)
                act_fn(EX[:], LX[:], ACT.Exp).then_inc(fin_exp, 1)
                split_hi(act, U_C, 8, h, 6)
                act.wait_ge(ktr_done, h + 1)
                act_fn(KETOK[:].rearrange("p a b -> p (a b)"), ps[:, 6, 0:3 * P], ACT.Copy).then_inc(ktok_ready, 1)
                split_hi(act, U_C, 8, h, 7)
                act.wait_ge(ro_done, h + 1)
                act_fn(OSQ[:], ps[:, 6, :], ACT.Square).then_inc(osq_ready, 1)
                act.wait_ge(omean_done, h + 1)
                act_fn(ORS[:], ps[:, 7, :], ACT.Sqrt, bias=eps[:, 0:1], scale=1.0 / P).then_inc(ostd_ready, 1)
                take(U_C + 8 * h + 8, 1, A1 + A2 + B_ + 2 * h + 1)

            for f in range(8):
                act.wait_ge(ot_done, f + 1)
                act_fn(OBH[:, f, :], ps[:, f, :], ACT.Copy).then_inc(act_hi, 1)
            act.wait_ge(oa_ready, 1 + H_A)
            for f in range(8):
                act_fn(OAH[:, f, :], OAF[:, f, :], ACT.Copy).then_inc(act_hi, 1)
            with act.Fori(0, D_ // 2) as i:
                for half in range(2):
                    for q in range(4):
                        split_hi(act, U_D, 8, i, 4 * half + q)
                        if q == 0:
                            act.wait_ge(mg_in[half], 32 * (i + 1))
                            act_fn(MG[:, half], MG[:, half], ACT.Sigmoid).then_inc(mg_ready, 1)
                    act.wait_ge(ms_ready, 1 + 2 * i + half + 1)
                    act_fn(XH[:, bass.ds(4 * i + 2 * half, 2), :], MS[:], ACT.Copy).then_inc(act_hi, 2)
            with act.Fori(0, E_ // 2) as i:
                for half in range(2):
                    for q in range(4):
                        split_hi(act, U_E, 8, i, 4 * half + q)
                    act.wait_ge(blk_taken, 1 + D_ + 2 * i + half + 2)
                    act_fn(SQ2[:], MIX[:, bass.ds(4 * i + 2 * half, 2), :], ACT.Square).then_inc(pair_sq, 1)
            act.wait_ge(mean_ready, 1)
            act_fn(RS1[:], ps[:, 6, :], ACT.Sqrt, bias=eps[:, 0:1], scale=1.0 / D).then_inc(std_ready, 1)
            for k in range(DT):
                act.wait_ge(h_ready, k + 1)
                if k >= 2:
                    act.wait_ge(sq_used, DT + k - 1)
                act_fn(SQ2[:, k % 2, :], HX[:, k, :], ACT.Square).then_inc(hsq_ready, 1)
            act.wait_ge(sq_used, 2 * DT)
            act_fn(RS2[:], ps[:, 7, :], ACT.Sqrt, bias=eps[:, 0:1], scale=1.0 / D).then_inc(std_ready, 1)
            halves_of(TN2, DT)

            j0 = D_ + E_

            def gate_up(u0, per, i, s0, half, job, place, pair):
                for q in range(8):
                    split_hi(act, u0, per, i, s0 + q)
                    if q == 3:
                        act.wait_ge(unit_done, 1 + u0 + per * i + s0 + 4)
                        act.wait_ge(hid_lo, 1 + 2 * pair)
                        act_fn(GT[:], ps[:, 4 * half:4 * half + 2, :], ACT.Silu).then_inc(silu_ready, 1)
                act.wait_ge(blk_taken, 1 + job + 2)
                act_fn(HH[:, place:place + 2, :], GT[:], ACT.Copy).then_inc(hid_hi, 1)

            gate_up(U_G, 0, 0, 0, 0, j0, 0, 0)
            gate_up(U_G, 0, 0, 8, 1, j0 + 1, 4, 1)
            with act.Fori(0, (PARTS - 1) // 2) as i:
                for half in range(2):
                    job = j0 + 2 + 20 * i + 10 * half
                    pair = 2 + 4 * i + 2 * half
                    gate_up(U_G1, 48, i, 24 * half, half, job, 2 * (1 - half), pair)
                    for q in range(8):
                        split_hi(act, U_G1, 48, i, 24 * half + 8 + q)
                    gate_up(U_G1, 48, i, 24 * half + 16, half, job + 9, 4, pair + 1)
            for c in range(8):
                if U_H + c + AHEAD < U_END:
                    split_hi(act, U_H, 0, 0, c)
                act.wait_ge(blk_taken, 1 + j0 + 2 + 10 * (PARTS - 1) + c + 2)
                if c:
                    act.wait_ge(ssum_ready, E_ + c)
                act_fn(SQ3[:], FFA[:, 2 * c:2 * c + 2, :], ACT.Square).then_inc(pair_sq, 1)
            act.wait_ge(mean_ready, 2)
            act_fn(RS3[:], ps[:, 6, :], ACT.Sqrt, bias=eps[:, 0:1], scale=1.0 / D).then_inc(std_ready, 1)

        @block.vector
        def _(dve):
            tt, ts, stt = nc.vector.tensor_tensor, nc.vector.tensor_scalar, nc.vector.scalar_tensor_tensor
            MUL, ADD, SUB, MAX = ALU.mult, ALU.add, ALU.subtract, ALU.max

            def then():
                dve.drain()

            dve.memset(ones[:], 1.0).then_inc(ones_ok, 1)
            dve.memset(eps[:], EPS).then_inc(ones_ok, 1)
            dve.wait_ge(vec_in, 16)

            def normalise(src, tn, rstd, gain, base, n_std):
                dve.wait_ge(std_ready, n_std)
                dve.reciprocal(rstd[:], rstd[:])
                then()
                if base == 0:
                    for s in range(-AHEAD, 0):
                        split_lo(dve, 0, 0, 0, s)
                for k in range(DT + 1):
                    if k < DT:
                        then()
                        stt(tn[:, k % 2, :], src[:, k, :], col(gain, k), rstd[:], MUL, MUL).then_inc(tn_ready, 1)
                    if k:
                        dve.wait_ge(act_hi, base + k)
                        tt(XL[:, k - 1, :], tn[:, (k - 1) % 2, :], XH[:, k - 1, :].bitcast(F32), SUB).then_inc(act_lo, 1)

            normalise(XS, TN, RSTD, V_PRE, 0, 1)
            dve.memset(cmpo[:], 0.0)
            dve.wait_ge(consts_in, 144)
            dve.tensor_copy(maskb[:], cload[:, 0:P])
            dve.tensor_copy(cmaskb[:], cload[:, P:2 * P])
            dve.tensor_copy(identb[:], ident[:])
            l0, l1 = vec[:, V_L0:V_L0 + H_A], vec[:, V_L1:V_L1 + H_A]
            tt(lbt[:, 2, :], l0, l1, MAX)
            then()
            tt(lbt[:, 0, :], l0, lbt[:, 2, :], SUB)
            tt(lbt[:, 1, :], l1, lbt[:, 2, :], SUB).then_inc(lb_shifted, 1)
            then()
            dve.memset(rsum[:], 0.0).then_inc(consts_ok, 1)
            dve.wait_ge(lb_exp, 1)
            tt(lbt[:, 1, :], lbt[:, 0, :], lbt[:, 1, :], ADD)
            then()
            dve.reciprocal(lbt[:, 1, :], lbt[:, 1, :])
            then()
            tt(lb[:], lbt[:, 0, :], lbt[:, 1, :], MUL)
            then()
            ts(olb[:], lb[:], -1.0, 1.0, MUL, ADD)

            dve.wait_ge(wg_hi_ok, 1)
            tt(wgl[:], wgf[:], wgh[:].bitcast(F32), SUB).then_inc(wg_lo_ok, 1)
            with dve.Fori(0, A1 // 2) as i:
                for s in range(8):
                    split_lo(dve, U_A1, 8, i, s)

            def blocks(x):
                dve.wait_ge(kd_in, 64 * (x + 1))
                if x:
                    dve.wait_ge(hid_done, 1)
                for kv in range(KV):
                    for jh in range(2):
                        o = tt(Rb[:, 8 * jh:8 * jh + 8, kv, :],
                               KD[:, kv, 16 * jh:16 * jh + 16 * CB].rearrange("p (n s) -> p s n", s=16)[:, 0:16:2, :],
                               pe2[:, x, 8 * jh:8 * jh + 8].unsqueeze(2).to_broadcast([P, 8, CB]), ADD)
                o.then_inc(blocks_ready, 1)

            for s in range(4 * A2):
                split_lo(dve, U_A2, 0, 0, s)
                if s in (2, 3):
                    if s == 2:
                        dve.wait_ge(kcs_in, 32)
                    for kv in (2 * s - 4, 2 * s - 3):
                        dve.wait_ge(krot_done, kv + 1)
                        bank = ps[:, 4 + kv % 2, :]
                        tt(bank, bank, kcs[:, 1, :], MUL)
                        tt(Kb[:, kv, :], Kb[:, kv, :], kcs[:, 0, :], MUL)
                        then()
                        tt(Kb[:, kv, :], Kb[:, kv, :], bank, ADD).then_inc(k_ready, 1)
                if s in (4, 9):
                    blocks((s - 4) // 5)
                if s == 9:
                    dve.wait_ge(crot_done, 1)
                    bank = ps[0:DH, 6, 0:KV * NC].rearrange("p (a b) -> p a b", a=KV)
                    cc, sc = (ccs[:, a, :].unsqueeze(1).to_broadcast([DH, KV, NC]) for a in range(2))
                    tt(bank, bank, sc, MUL)
                    tt(KC[:], cmpo[:], cc, MUL)
                    then()
                    tt(KC[:], KC[:], bank, ADD).then_inc(kc_ready, 1)
            dve.wait_ge(qcs_in, 16)
            dve.wait_ge(gates_ready, 1)
            dve.wait_ge(vc_ready, 1)
            dve.wait_ge(v_ready, 4)
            dve.memset(rsum[:], 0.0).then_inc(q_ready, 1)

            dve.memset(QR[:], 0.0)
            then()
            with dve.Fori(0, KV) as kv:
                dve.wait_ge(q_in, 64 * (kv + 1))
                for g in range(GRP):
                    hd = GRP * kv + g

                    def maxima(k):
                        dve.wait_ge(s_done, 9 * hd + k + 1)
                        if k:
                            n = P * ((k - 1) // 2 + 1)
                            nc.vector.tensor_reduce(negmax[:, k % 2:k % 2 + 1], ps[:, 4 + k % 2, 0:n], AX.X, MAX,
                                                    negate=True).then_inc(max_ready, 1)
                            return
                        s = ps[:, 4, 0:NT * NC].rearrange("p (a b) -> p a b", a=NT)
                        nc.vector.tensor_reduce(cstat[:, 0, :], s, AX.X, MAX)
                        then()
                        tt(PC[:], s, cstat[:, 0, :].unsqueeze(2).to_broadcast([P, NT, NC]), SUB).then_inc(max_ready, 1)

                    def weigh(k):
                        dve.wait_ge(exp_done, 1 + 9 * hd + k + 1)
                        if k:
                            b, t_ = (k - 1) % 2, (k - 1) // 2
                            n = P * (t_ + 1)
                            r = slice(k % 2, k % 2 + 1)
                            dve.reciprocal(rsum[:, r], expsum[:, r])
                            then()
                            ts(rsum[:, r], rsum[:, r], gates[:, t_, bass.ds(3 * hd + 1 + b, 1)], None, MUL)
                            then()
                            ts(Pb[:, k % 2, 0:n], Pb[:, k % 2, 0:n], rsum[:, r], None, MUL).then_inc(p_ready, 1)
                            return
                        nc.vector.tensor_reduce(cstat[:, 1, :], PC[:], AX.X, ADD)
                        then()
                        tt(PC[:], PC[:], c01[:], MUL)
                        dve.reciprocal(cstat[:, 1, :], cstat[:, 1, :])
                        then()
                        tt(cstat[:, 2, :], cstat[:, 1, :], gates[:, :, bass.ds(3 * hd, 1)].rearrange("p a b -> p (a b)"), MUL)
                        then()
                        tt(PC[:], PC[:], cstat[:, 2, :].unsqueeze(2).to_broadcast([P, NT, NC]), MUL).then_inc(p_ready, 1)

                    split_lo(dve, U_B, 16, kv, 4 * g)
                    dve.wait_ge(qrot_done, hd + 1)
                    tt(ps[:, 4, :], ps[:, 4, :], qcs[:, 1, :], MUL)
                    tt(Qb[:, hd, :], Qb[:, hd, :], qcs[:, 0, :], MUL)
                    then()
                    for b, rows in enumerate((slice(0, DH), slice(DH, P))):
                        o = tt(QR[rows, b, :], Qb[rows, hd, :], ps[rows, 4, :], ADD)
                    o.then_inc(q_ready, 1)
                    maxima(0)
                    weigh(0)
                    split_lo(dve, U_B, 16, kv, 4 * g + 1)
                    maxima(1)
                    for k in (2, 3, 4):
                        maxima(k)
                        weigh(k - 1)
                    split_lo(dve, U_B, 16, kv, 4 * g + 2)
                    for k in (5, 6, 7, 8):
                        maxima(k)
                        weigh(k - 1)
                    split_lo(dve, U_B, 16, kv, 4 * g + 3)
                    weigh(8)
                    dve.wait_ge(v_done, 1 + 8 * hd + 8)
                    dve.tensor_copy(otok[:, :, bass.ds(hd * DH, DH)],
                                    ps[:, 7, 0:NT * DH].rearrange("p (a b) -> p a b", a=NT)).then_inc(o_ready, 1)

            dve.wait_ge(lm_in, 16)
            dve.memset(QT[:], 0.0)
            dve.memset(KT[:], 0.0)
            dve.memset(ATT[:], 0.0)
            then()
            with dve.Fori(0, H_A) as h:
                def decayed(lev):
                    w = 1 << (lev - 1)
                    if lev >= 3:
                        dve.wait_ge(lev_done, 8 * h + lev - 1)
                    dve.wait_ge(dec_done, 7 * h + lev)
                    b = lev % 2
                    tt(halves(QT[:, b], w)[1], halves(LQ, w)[1], flat(EQ, w), MUL)
                    tt(halves(KT[:, b], w)[0], halves(KF, w)[0], flat(EK, w), MUL).then_inc(qk_ready, 1)
                    (p_lo, p_up), (x_lo, x_up) = halves(LP, w), halves(LX, w)
                    shape = [P, T // (2 * w), w]
                    tt(x_lo, x_lo, p_up[:, :, w - 1:w].to_broadcast(shape), ADD)
                    then()
                    tt(p_up, p_up, p_lo[:, :, w - 1:w].to_broadcast(shape), ADD).then_inc(px_ready, 1)

                def keep(lev):
                    dve.wait_ge(lev_done, 8 * h + lev + 1)
                    dve.memset(waited[:, lev:lev + 1], 0.0)
                    nc.vector.copy_predicated(ATT[:], lmask[:, lev, :].bitcast(U32).unsqueeze(1).to_broadcast([P, NT, P]),
                                              ps[:, 4 + lev % 2, :].rearrange("p (a b) -> p a b", a=NT)).then_inc(att_taken, 1)

                split_lo(dve, U_C, 8, h, 0)
                dve.memset(LX[:], 0.0).then_inc(px_ready, 1)
                dve.wait_ge(sig_done, h + 1)
                ts(SIG[:], SIG[:], olb[:, bass.ds(h, 1)], lb[:, bass.ds(h, 1)], MUL, ADD)
                then()
                ts(KF[:], SIG[:], -1.0, 1.0, MUL, ADD).then_inc(f_ready, 1)
                dve.wait_ge(sgm_done, h + 1)
                tt(SG[:], SGM[:], LG[:], MUL).then_inc(sg_ready, 1)
                dve.wait_ge(q_ld, 16 * (h + 1))
                decayed(1)
                split_lo(dve, U_C, 8, h, 1)
                keep(0)
                decayed(2)
                keep(1)
                split_lo(dve, U_C, 8, h, 2)
                decayed(3)
                keep(2)
                decayed(4)
                split_lo(dve, U_C, 8, h, 3)
                keep(3)
                decayed(5)
                split_lo(dve, U_C, 8, h, 4)
                keep(4)
                decayed(6)
                keep(5)
                split_lo(dve, U_C, 8, h, 5)
                decayed(7)
                keep(6)
                dve.wait_ge(fin_exp, h + 1)
                tt(QE[:], LQ[:], EB[:], MUL)
                tt(KE[:], KF[:], EX[:], MUL).then_inc(fin_ready, 1)
                split_lo(dve, U_C, 8, h, 6)
                then()
                keep(7)
                split_lo(dve, U_C, 8, h, 7)
                dve.wait_ge(g_done, h + 1)
                dve.tensor_copy(ST[:, 0, :], ps[:, 7, 0:P])
                for c in (1, 2):
                    then()
                    o = stt(ST[:, c, :], ST[:, c - 1, :], EB[:, c * P + P - 1:c * P + P], ps[:, 7, c * P:c * P + P], MUL, ADD)
                o.then_inc(st_ready, 1)
                dve.wait_ge(ostd_ready, h + 1)
                dve.reciprocal(ORS[:], ORS[:])
                then()
                stt(OSQ[:], ps[:, 6, :], vec[:, bass.ds(V_AN + h, 1)], ORS[:], MUL, MUL)
                then()
                tt(OAF[:, h, :], OSQ[:], SG[:], MUL).then_inc(oa_ready, 1)

            for f in range(8):
                dve.wait_ge(act_hi, DT + f + 1)
                tt(OBL[:, f, :], ps[:, f, :], OBH[:, f, :].bitcast(F32), SUB).then_inc(act_lo, 1)
            for f in range(8):
                dve.wait_ge(act_hi, DT + 8 + f + 1)
                tt(OAL[:, f, :], OAF[:, f, :], OAH[:, f, :].bitcast(F32), SUB).then_inc(act_lo, 1)
            with dve.Fori(0, D_ // 2) as i:
                for half in range(2):
                    for q in range(4):
                        split_lo(dve, U_D, 8, i, 4 * half + q)
                    then()
                    dve.wait_ge(mg_ready, 2 * i + half + 1)
                    dve.wait_ge(unit_done, 1 + U_D + 8 * i + 4 * half + 4)
                    dve.wait_ge(act_hi, DT + 16 + 4 * i + 2 * half)
                    tt(MT[:], MG[:, half, 0:2, :], ps[:, 4 * half:4 * half + 2, :], MUL)
                    tt(MS[:], MG[:, half, 2:4, :], ps[:, 4 * half + 2:4 * half + 4, :], MUL).then_inc(blk_taken, 1)
                    then()
                    tt(MS[:], MS[:], MT[:], ADD).then_inc(ms_ready, 1)
                    dve.wait_ge(act_hi, DT + 16 + 4 * i + 2 * half + 2)
                    f = bass.ds(4 * i + 2 * half, 2)
                    tt(XL[:, f, :], MS[:], XH[:, f, :].bitcast(F32), SUB).then_inc(act_lo, 2)

            def add_squares(total, sq, n):
                then()
                dve.wait_ge(pair_sq, n + 1)
                tt(total[:], total[:], sq[:, 0, :], ADD)
                then()
                tt(total[:], total[:], sq[:, 1, :], ADD).then_inc(ssum_ready, 1)

            dve.memset(SACC[:], 0.0)
            with dve.Fori(0, E_ // 2) as i:
                for half in range(2):
                    for q in range(4):
                        split_lo(dve, U_E, 8, i, 4 * half + q)
                    dve.wait_ge(unit_done, 1 + U_E + 8 * i + 4 * half + 4)
                    dve.tensor_copy(MIX[:, bass.ds(4 * i + 2 * half, 2), :], ps[:, 4 * half:4 * half + 2, :]).then_inc(blk_taken, 1)
                    add_squares(SACC, SQ2, 2 * i + half)
            dve.wait_ge(std_ready, 2)
            dve.reciprocal(RS1[:], RS1[:])
            dve.wait_ge(hx_in, 64)
            for k in range(DT + 1):
                then()
                if k < DT:
                    stt(TN2[:, k % 2, :], MIX[:, k, :], col(V_POST, k), RS1[:], MUL, MUL)
                if k:
                    tt(HX[:, k - 1, :], HX[:, k - 1, :], TN2[:, (k - 1) % 2, :], ADD).then_inc(h_ready, 1)
            normalise(HX, TN2, RS2, V_PREF, DT + 32, 3)

            j0 = D_ + E_

            def gate_up(u0, per, i, s0, half, place, pair):
                for q in range(8):
                    split_lo(dve, u0, per, i, s0 + q)
                dve.wait_ge(unit_done, 1 + u0 + per * i + s0 + 8)
                dve.wait_ge(silu_ready, pair + 1)
                tt(GT[:], GT[:], ps[:, 4 * half + 2:4 * half + 4, :], MUL).then_inc(blk_taken, 1)
                dve.wait_ge(hid_hi, pair + 1)
                tt(HL[:, place:place + 2, :], GT[:], HH[:, place:place + 2, :].bitcast(F32), SUB).then_inc(hid_lo, 2)

            def add_part(u_end, bank, c):
                then()
                dve.wait_ge(unit_done, 1 + u_end)
                tt(FFA[:, 2 * c:2 * c + 2, :], FFA[:, 2 * c:2 * c + 2, :], ps[:, bank:bank + 2, :], ADD).then_inc(blk_taken, 1)

            dve.memset(FFA[:], 0.0)
            gate_up(U_G, 0, 0, 0, 0, 0, 0)
            gate_up(U_G, 0, 0, 8, 1, 4, 1)
            with dve.Fori(0, (PARTS - 1) // 2) as i:
                for half in range(2):
                    pair = 2 + 4 * i + 2 * half
                    gate_up(U_G1, 48, i, 24 * half, half, 2 * (1 - half), pair)
                    for c in range(8):
                        split_lo(dve, U_G1, 48, i, 24 * half + 8 + c)
                        add_part(U_G1 + 48 * i + 24 * half + 9 + c, 4 * (1 - half) + 2 * (c % 2), c)
                    gate_up(U_G1, 48, i, 24 * half + 16, half, 4, pair + 1)
            dve.memset(SACC2[:], 0.0)
            for c in range(8):
                if U_H + c + AHEAD < U_END:
                    split_lo(dve, U_H, 0, 0, c)
                add_part(U_H + c + 1, 2 * (c % 2), c)
                add_squares(SACC2, SQ3, E_ + c)
            dve.wait_ge(std_ready, 4)
            dve.reciprocal(RS3[:], RS3[:])
            for k in range(DT + 1):
                then()
                if k < DT:
                    stt(FFA[:, k, :], FFA[:, k, :], col(V_POSTF, k), RS3[:], MUL, MUL)
                if k:
                    tt(FFA[:, k - 1, :], FFA[:, k - 1, :], HX[:, k - 1, :], ADD).then_inc(out_ready, 1)


def chunks(w, n):
    k = w.shape[0] // P
    return np.ascontiguousarray(w.reshape(k, P, n, CH).transpose(2, 1, 0, 3).reshape(n, P, k * CH))


def by_tile(v):
    return v.reshape(-1, P).T


def shape_constants():
    half = 8
    inv = np.float32(500000.0) ** (-np.arange(half, dtype=np.float32) * np.float32(2.0) / np.float32(16))

    def tables(pos, scale):
        ang = pos.astype(np.float32)[:, None] * inv[None, :]
        c, s = np.ones((DH, len(pos)), np.float32), np.zeros((DH, len(pos)), np.float32)
        c[0:half] = c[half:2 * half] = np.cos(ang).T
        s[0:half] = s[half:2 * half] = np.sin(ang).T
        return c * np.float32(scale), s * np.float32(scale)

    k = np.zeros((P, K_N), np.float32)
    k[:, K_ID:K_ID + P] = np.eye(P)
    for base in (0, DH):
        for i in range(half):
            k[base + half + i, K_ROT + base + i] = -1.0
            k[base + i, K_ROT + base + half + i] = 1.0
    q, c = np.arange(P)[:, None], np.arange(P)[None, :]
    k[:, K_DIAG:K_DIAG + P] = np.where(c > q, NEG, 0.0)
    t = q + P * np.arange(NT).repeat(NC)[None, :]
    n = np.tile(np.arange(NC), NT)[None, :]
    seen = (16 * n + CB <= t) & (n < CB)
    k[:, K_CM:K_CM + P] = np.where(seen, 0.0, NEG)
    k[:, K_C01:K_C01 + P] = seen
    for at_, pos, scale in (((K_CQ, K_SQ), np.arange(T), DH ** -0.5), ((K_CK, K_SK), np.arange(T), 1.0),
                            ((K_CC, K_SC), np.arange(NC) * 16 + CB, 1.0)):
        for a, tab in zip(at_, tables(pos, scale)):
            k[0:DH, a:a + len(pos)] = k[DH:P, a:a + len(pos)] = tab
    masks = np.zeros((P, LEVELS, P), np.float32)
    s, t = np.arange(P)[:, None], np.arange(P)[None, :]
    masks[:, 0, :] = s == t
    for lev in range(1, LEVELS):
        w = 1 << (lev - 1)
        masks[:, lev, :] = (s // (2 * w) == t // (2 * w)) & (s % (2 * w) < w) & (t % (2 * w) >= w)
    return k, masks.reshape(P, LEVELS * P)


def kernel(**inputs):
    import concourse.bacc as bacc
    from concourse.bass_utils import run_bass_kernel_spmd

    a = {n: np.asarray(v) for n, v in inputs.items()}
    w_in = a["w_in"][0]
    kv = [w_in[:, 5120 + CH * j:5120 + CH * j + CH] for j in range(6)]
    consts, masks = shape_constants()
    arrays = {
        "x_t": np.ascontiguousarray(a["x"][0].T).reshape(DT, P, T),
        "w_a": chunks(np.concatenate(kv + [w_in[:, 4096:5120]], axis=1), A1 + A2),
        "w_b": chunks(w_in[:, 0:4096], B_),
        "w_c": chunks(w_in[:, 6704:10800], C_),
        "w_d": np.concatenate([chunks(a["w_proj_a"][0], D_), chunks(a["w_proj_b"][0], D_)], axis=2),
        "w_e": chunks(a["w_out"][0], E_),
        "w_g": np.concatenate([chunks(a["w_gate"][0], FF // CH), chunks(a["w_up"][0], FF // CH)], axis=2),
        "w_h": np.ascontiguousarray(a["w_down"][0].reshape(PARTS, KU, P, 8, CH).transpose(0, 2, 3, 1, 4)
                                    .reshape(PARTS, P, 8 * UN)),
        "w_gate": np.ascontiguousarray(w_in[:, 6656:6704].reshape(DT, P, 48).transpose(1, 0, 2)),
        "vecs": np.ascontiguousarray(np.concatenate([by_tile(v) for v in (
            a["pre_mix_g"][0], a["post_mix_g"][0], a["pre_ffn_g"][0], a["post_ffn_g"][0], a["a_norm_g"][0],
            a["lb_table"][0], a["lb_table"][1], a["cmp_b1_k"][0], a["cmp_b1_v"][0])], axis=1)),
        "consts": consts,
        "level_mask": masks,
    }
    for x in ("k", "v"):
        arrays["pe_" + x] = np.ascontiguousarray(a["cmp_pe_" + x][0].reshape(16, P).T)
    for x in ("k", "v"):
        arrays["w1_" + x] = np.ascontiguousarray(a["cmp_w1_" + x][0].reshape(16, P, CH).transpose(1, 0, 2))
    for x in ("k", "v"):
        arrays["w2_" + x] = np.ascontiguousarray(a["cmp_w2_" + x][0].reshape(2, P, DH).transpose(1, 0, 2))
    arrays["b2"] = np.ascontiguousarray(np.stack([a["cmp_b2_k"][0], a["cmp_b2_v"][0]], axis=1))

    nc = bacc.Bacc("TRN2", target_bir_lowering=False, num_devices=1)
    args = [nc.dram_tensor("in_" + n, v.shape, mybir.dt.from_np(v.dtype), kind="ExternalInput").ap()
            for n, v in arrays.items()]
    res = nc.dram_tensor("out_t", [DT, P, T], F32, kind="ExternalOutput").ap()
    hybrid_block(nc, *args, res)
    r = run_bass_kernel_spmd(nc, [{"in_" + n: v for n, v in arrays.items()}], core_ids=[0])
    return np.ascontiguousarray(r.results[0]["out_t"].reshape(D, T).T)[None]
```

```python
from contextlib import ExitStack

import numpy as np
import concourse.bass as bass
from concourse import mybir

F32 = mybir.dt.float32
F32R = mybir.dt.float32r
BF16 = mybir.dt.bfloat16
U32 = mybir.dt.uint32
ALU = mybir.AluOpType
ACT = mybir.ActivationFunctionType
AX = mybir.AxisListType

P = 128
T = 512
D = 2048
DT = D // P
FF = 5632
FT = FF // P
NT = T // P
CH = 256
KU = 4
UN = KU * CH
RING = 4
AHEAD = 3
H_A = 8
H_B = 16
KV = 4
GRP = H_B // KV
DH = 64
NC = 32
CB = 31
LEVELS = 8
EPS = 1e-6
NEG = -1e30

KB = 1024
BASE = 16512
XREG = BASE + 48 * KB
Z = BASE + 112 * KB
TOP = BASE + 204 * KB

A1, A2, B_, C_ = 6, 4, 16, 16
D_, E_ = 8, 8
PARTS = FT // KU
U_A1 = 0
U_A2 = U_A1 + 4 * A1
U_B = U_A2 + 4 * A2
U_C = U_B + 4 * B_
U_D = U_C + 4 * C_
U_E = U_D + 4 * D_
U_G = U_E + 4 * E_
U_G1 = U_G + 16
U_H = U_G1 + 24 * (PARTS - 1)
U_END = U_H + 8
TILE_KC, TILE_VC, TILE_KS, TILE_VS, TILE_KW, TILE_VW, TILE_Q = 0, 2, 4, 6, 8, 10, 12
TILE_HQ, TILE_HF, TILE_HI, TILE_HG, TILE_MA, TILE_MB = 20, 28, 36, 44, 52, 68
V_PRE, V_POST, V_PREF, V_POSTF, V_AN, V_L0, V_L1, V_B1K, V_B1V = 0, 16, 32, 48, 64, 72, 80, 88, 90
V_N = 92
K_ID, K_ROT, K_DIAG, K_CM, K_C01, K_CQ, K_SQ, K_CK, K_SK, K_CC, K_SC = (
    0, 128, 256, 384, 512, 640, 1152, 1664, 2176, 2688, 2720)
K_N = 2752


def hybrid_block(nc, x_t, w_a, w_b, w_c, w_d, w_e, w_g, w_h, w_gate, vecs, consts, level_mask,
                 pe_k, pe_v, w1_k, w1_v, w2_k, w2_v, b2, out):
    with ExitStack() as ctx:
        def at(name, shape, dt, where):
            return nc.alloc_sbuf_tensor_at(name, shape, dt, offset=int(where))

        def sem(name):
            return ctx.enter_context(nc.semaphore(name))

        proj = nc.dram_tensor("proj_scratch", [84, P, T], F32, kind="Internal").ap()
        hscr = nc.dram_tensor("h_scratch", [DT, P, T], F32, kind="Internal").ap()

        raw = [at(f"w_raw{r}", [P, UN], F32, BASE + 4 * KB * r) for r in range(RING)]
        whi = [at(f"w_hi{r}", [P, UN], F32R, BASE + 16 * KB + 4 * KB * r) for r in range(RING)]
        wlo = [at(f"w_lo{r}", [P, UN], F32R, BASE + 32 * KB + 4 * KB * r) for r in range(RING)]
        XH = at("act_hi", [P, DT, T], F32R, XREG)
        XL = at("act_lo", [P, DT, T], F32R, XREG + 32 * KB)
        ident = at("ident", [P, P], F32, TOP)
        ones = at("ones", [P, P], F32, TOP + 512)
        vec = at("vec", [P, V_N], F32, TOP + 1024)
        eps = at("eps", [P, 1], F32, TOP + 1536)
        lb = at("lb", [P, H_A], F32, TOP + 1568)
        olb = at("one_minus_lb", [P, H_A], F32, TOP + 1600)
        pe2 = at("pe2", [P, 2, 16], F32, TOP + 1632)
        w2s = at("w2s", [P, 2, 2, DH], F32, TOP + 1760)
        b2s = at("b2s", [DH, 2], F32, TOP + 2784)
        negmax = at("negmax", [P, 2], F32, TOP + 2816)
        expsum = at("expsum", [P, 2], F32, TOP + 2848)
        rsum = at("rsum", [P, 2], F32, TOP + 2880)
        cstat = at("cstat", [P, 3, 4], F32, TOP + 2912)
        waited = at("waited", [P, LEVELS], F32, TOP + 3616)
        rtok = at("rstd_by_token", [P, NT], F32, TOP + 3936)
        c01 = at("cmp_mask01", [P, 4, NC], F32, TOP + 3072)
        XS = at("x_in", [P, DT, T], F32, Z)
        DG = at("rstd_diag", [P, NT, P], F32, Z + 44 * KB)
        RSTD = at("rstd_x", [P, T], F32, Z + 82 * KB)
        cload = at("const_load", [P, 256], F32, Z + 52 * KB)
        lbt = at("lb_tmp", [P, 3, H_A], F32, Z + 54 * KB)
        Kb = at("keys", [P, KV, T], F32, Z)
        Vb = at("values", [P, 2, NT, KV * DH], F32, Z + 8 * KB)
        Qb = at("queries", [P, GRP, T], F32, Z + 16 * KB)
        Qs = at("queries_swapped", [P, GRP, T], F32, Z + 24 * KB)
        wgf = at("wg_f", [P, DT, 48], F32, Z + 16 * KB)
        wgh = at("wg_hi", [P, DT, 48], F32R, Z + 19 * KB)
        wgl = at("wg_lo", [P, DT, 48], F32R, Z + 22 * KB)
        GL = at("gate_logits", [48, T], F32, Z + 88 * KB)
        kcs = at("rope_k", [P, 2, T], F32, Z + 36 * KB)
        Vst = at("v_stage", [P, 2, 2, T], F32, Z + 40 * KB)
        KD = at("cmp_in", [P, KV, T], F32, Z + 48 * KB)
        Rb = at("cmp_blocks", [P, 16, KV, CB], F32, Z + 56 * KB)
        otok = at("attn_out", [P, NT, H_B * DH], F32, Z + 48 * KB)
        KC = at("k_cmp", [DH, KV, NC], F32, Z + 64 * KB)
        VC = at("v_cmp", [NC, KV, DH], F32, Z + 64 * KB + 512)
        rot = at("rot", [P, P], F32, Z + 65 * KB + 512)
        w1s = at("w1s", [P, 16, CH], F32, Z + 66 * KB)
        ccs = at("rope_cmp", [DH, 2, NC], F32, Z + 32 * KB + 768)
        qcs = at("rope_q", [P, 2, T], F32, Z + 66 * KB)
        QR = at("q_rot", [P, 2, T], F32, Z + 88 * KB)
        Pb = at("probs", [P, 2, T], F32, Z + 72 * KB)
        PT = at("probs_t", [P, 2, T], F32, Z + 76 * KB)
        PC = at("probs_cmp", [P, 4, NC], F32, Z + 80 * KB)
        PCT = at("probs_cmp_t", [NC, T], F32, Z + 40 * KB)
        VG = at("group_values", [P, 2, NT, DH], F32, Z + 70 * KB)
        VCG = at("group_v_cmp", [NC, DH], F32, TOP + 3680)
        maskb = at("diag_mask", [P, P], BF16, Z + 32 * KB)
        cmaskb = at("cmp_mask", [P, P], BF16, Z + 32 * KB + 256)
        gates = at("gates", [P, NT, 48], F32, Z + 33 * KB)
        identb = at("ident_bf", [P, P], BF16, Z + 32 * KB + 512)
        OS = at("out_stage", [P, 2, T], F32, Z + 84 * KB)
        HG = at("cmp_hidden", [P, 2, KV * CB], F32, Z + 34 * KB)
        cmpo = at("cmp_out", [DH, KV, NC], F32, Z + 35 * KB)
        SIG, LP, LX = [at(n, [P, T], F32, Z + 8 * KB + 2 * KB * i) for i, n in enumerate(["sig", "prefix", "suffix"])]
        QT = at("q_decayed", [P, 2, T // 2], F32, Z + 14 * KB)
        KT = at("k_decayed", [P, 2, T], F32, Z + 18 * KB)
        EQ = at("decay_q", [P, T // 2], F32, Z + 22 * KB)
        EK = at("decay_k", [P, T // 2], F32, Z + 23 * KB)
        ATT = at("att_t", [P, NT, P], F32, Z + 24 * KB)
        ITOK = at("i_tok", [P, NT, P], F32, Z + 26 * KB)
        KETOK = at("k_tok", [P, 3, P], F32, Z + 28 * KB)
        ST = at("state", [P, 3, P], F32, Z + 30 * KB)
        SG, OSQ, ORS, KF = [at(n, [P, T], F32, Z + 2 * KB * i) for i, n in enumerate(["silu_g", "o_sq", "o_rstd", "k_f"])]
        EB, LQ, LF, LI, EX, LG, QE, KE = [at(n, [P, T], F32, Z + 32 * KB + 2 * KB * i) for i, n in enumerate(
            ["decay_all", "in_q", "in_f", "in_i", "decay_rest", "in_g", "q_all", "k_rest"])]
        lmask = at("level_masks", [P, LEVELS, P], F32, Z + 88 * KB)
        SGM = at("sig_g", [P, T], F32, Z + 64 * KB)
        OAF = at("oa", [P, H_A, T], F32, Z + 66 * KB)
        OAH, OAL, OBH = [at(n, [P, 8, T], F32R, Z + 16 * KB * i) for i, n in enumerate(["oa_hi", "oa_lo", "ob_hi"])]
        OBL = at("ob_lo", [P, 8, T], F32R, Z + 66 * KB)
        MG = at("merge_gates", [P, 2, 4, T], F32, Z + 48 * KB)
        MT = at("merge_tmp", [P, 2, T], F32, Z + 83 * KB)
        MS = at("merged", [P, 2, T], F32, Z + 87 * KB)
        MIX = at("mix", [P, DT, T], F32, Z)
        HX = at("residual", [P, DT, T], F32, Z + 32 * KB)
        SQ2 = at("squares2", [P, 2, T], F32, Z + 64 * KB)
        SACC = at("square_sum", [P, T], F32, Z + 68 * KB)
        RS1 = at("rstd_mix", [P, T], F32, Z + 70 * KB)
        DG2 = at("rstd_diag2", [P, NT, P], F32, Z + 72 * KB)
        TN2 = at("normed2", [P, 2, T], F32, Z + 74 * KB)
        FFA = at("ffn_sum", [P, DT, T], F32, Z)
        HH = at("hidden_hi", [P, 6, T], F32R, Z + 64 * KB)
        HL = at("hidden_lo", [P, 6, T], F32R, Z + 76 * KB)
        HV = at("hidden", [P, 6, T], F32, Z + 76 * KB)
        RS2 = at("rstd_h", [P, T], F32, Z + 88 * KB)
        SACC2 = at("square_sum2", [P, T], F32, XREG)
        RS3 = at("rstd3", [P, T], F32, XREG + 2 * KB)
        SQ3 = at("squares3", [P, 2, T], F32, XREG + 4 * KB)
        DG3 = at("rstd_diag3", [P, NT, P], F32, XREG + 8 * KB)

        ps = ctx.enter_context(nc.psum_tensor("ps", [P, 8, T], F32))

        landed = [sem(f"unit_landed{r}") for r in range(RING)]
        hi_ready, lo_ready, unit_done = sem("hi_ready"), sem("lo_ready"), sem("unit_done")
        x_in = [sem(f"x_in{i}") for i in range(DT // 2)]
        vec_in, consts_in, ones_ok, consts_ok = sem("vec_in"), sem("consts_in"), sem("ones_ok"), sem("consts_ok")
        sq_ready, mean_ready, std_ready, diag_ready, row_done, row_ready = (sem(n) for n in (
            "sq_ready", "mean_ready", "std_ready", "diag_ready", "row_done", "row_ready"))
        act_hi, act_lo, mean_scaled, ffn_clear = sem("act_hi"), sem("act_lo"), sem("mean_scaled"), sem("ffn_clear")
        proj_taken = sem("proj_taken")
        stored = sem("proj_stored")
        kraw_in, kcs_in, vst_in, w1_in, kd_in, q_in, qcs_in = (sem(n) for n in (
            "kraw_in", "kcs_in", "vst_in", "w1_in", "kd_in", "q_in", "qcs_in"))
        krot_done, k_ready, vt_done, v_ready, vg_ready, qs_clear = (sem(n) for n in (
            "krot_done", "k_ready", "vt_done", "v_ready", "vg_ready", "qs_clear"))
        blocks_ready, hid_done, gelu_done, cmp_done, cmp_biased, crot_done, kc_ready, vct_done, vc_ready = (
            sem(n) for n in ("blocks_ready", "hid_done", "gelu_done", "cmp_done", "cmp_biased", "crot_done",
                             "kc_ready", "vct_done", "vc_ready"))
        wg_in, wg_hi_ok, wg_lo_ok, glog_done, glog_out, glog_turned, gates_ready = (sem(n) for n in (
            "wg_in", "wg_hi_ok", "wg_lo_ok", "glog_done", "glog_out", "glog_turned", "gates_ready"))
        q_ready, s_done, max_ready, exp_done, p_ready, t_done, pt_ready, v_done, o_ready = (
            sem(n) for n in ("q_ready", "s_done", "max_ready", "exp_done", "p_ready", "t_done",
                             "pt_ready", "v_done", "o_ready"))
        lm_in, q_ld, f_ld, i_ld, g_ld = (sem(n) for n in ("lm_in", "q_ld", "f_ld", "i_ld", "g_ld"))
        sig_done, f_ready, ln_done, sgm_done, sg_ready, itr_done, itok_ready = (sem(n) for n in (
            "sig_done", "f_ready", "ln_done", "sgm_done", "sg_ready", "itr_done", "itok_ready"))
        dec_done, qk_ready, px_ready, lev_done, att_taken = (sem(n) for n in (
            "dec_done", "qk_ready", "px_ready", "lev_done", "att_taken"))
        fin_exp, fin_ready, ktr_done, ktok_ready, g_done, st_ready, ro_done, osq_ready, omean_done, ostd_ready, oa_ready = (
            sem(n) for n in ("fin_exp", "fin_ready", "ktr_done", "ktok_ready", "g_done", "st_ready", "ro_done",
                             "osq_ready", "omean_done", "ostd_ready", "oa_ready"))
        ot_done, mg_ready = sem("ot_done"), sem("mg_ready")
        mg_in = [sem(f"mg_in{i}") for i in range(2)]
        blk_taken, ms_ready = sem("blk_taken"), sem("ms_ready")
        pair_sq, ssum_ready, hx_in, h_ready = (sem(n) for n in ("pair_sq", "ssum_ready", "hx_in", "h_ready"))
        gate_ready, silu_ready, hid_hi, hid_lo, out_ready, out_done = (sem(n) for n in (
            "gate_ready", "silu_ready", "hid_hi", "hid_lo", "out_ready", "out_done"))
        lb_shifted, lb_exp = sem("lb_shifted"), sem("lb_exp")

        block = ctx.enter_context(nc.Block())

        def col(v, k):
            return vec[:, v + k:v + k + 1]

        def halves(t, w):
            v = t[:].rearrange("p (b h w) -> p b h w", h=2, w=w)
            return v[:, :, 0, :], v[:, :, 1, :]

        def flat(t, w):
            return t[:].rearrange("p (b w) -> p b w", w=w)

        @block.sync
        def _(sp):
            def load(u0, per, i, s, src, wait=True):
                u = u0 + per * i + s
                if wait:
                    sp.wait_ge(lo_ready, u - RING + 1)
                sp.dma_start(raw[(u0 + s) % RING][:], src).then_inc(landed[(u0 + s) % RING], 16)

            def cut(w, c, k):
                return w[c][:, k * UN:(k + 1) * UN]

            for s in range(8):
                if s % 2 == 0:
                    for k in (2 * s, 2 * s + 2):
                        sp.dma_start(XS[:, k:k + 2, :], x_t[k:k + 2].rearrange("k p t -> p k t")).then_inc(x_in[k // 2], 16)
                load(0, 0, 0, s, cut(w_a, s % 2, s // 2), wait=s >= RING)
            with sp.Fori(1, A1 // 2) as i:
                for s in range(8):
                    load(U_A1, 8, i, s, cut(w_a, 2 * i + s // 4, s % 4))
            for s in range(4 * A2):
                load(U_A2, 0, 0, s, cut(w_a, A1 + s // 4, s % 4))
            for u0, w, n in ((U_B, w_b, B_), (U_C, w_c, C_), (U_D, w_d, D_), (U_E, w_e, E_)):
                with sp.Fori(0, n // 2) as i:
                    for s in range(8):
                        load(u0, 8, i, s, cut(w, 2 * i + s // 4, s % 4))
            for s in range(8):
                load(U_G, 0, 0, s, cut(w_g, 0, 4 * (s % 2) + s // 2))
            for s in range(8):
                load(U_G, 0, 0, 8 + s, cut(w_g, 1, s))
            with sp.Fori(0, (PARTS - 1) // 2) as i:
                for half in range(2):
                    for s in range(8):
                        load(U_G1, 48, i, 24 * half + s, cut(w_g, 4 * i + 2 * half + 2, s))
                    for s in range(8):
                        load(U_G1, 48, i, 24 * half + 8 + s, cut(w_h, 2 * i + half, s))
                    for s in range(8):
                        load(U_G1, 48, i, 24 * half + 16 + s, cut(w_g, 4 * i + 2 * half + 3, s))
            for s in range(8):
                load(U_H, 0, 0, s, cut(w_h, PARTS - 1, s))
            for k in range(0, DT, 4):
                sp.wait_ge(out_ready, k + 4)
                sp.dma_start(out[k:k + 4].rearrange("k p t -> p k t"), FFA[:, k:k + 4, :]).then_inc(out_done, 16)
            sp.wait_ge(out_done, 16 * (DT // 4))

        @block.gpsimd
        def _(pool):
            for s in (exp_done, pt_ready, v_done, t_done, o_ready, unit_done, att_taken, oa_ready, ms_ready, hid_lo, ostd_ready,
                      proj_taken, proj_taken, blk_taken, blk_taken):
                pool.sem_inc(s, 1)
            pool.dma_start(vec[:], vecs).then_inc(vec_in, 16)
            pool.dma_start(cload[:, 0:256], consts[:, K_DIAG:K_DIAG + 256]).then_inc(consts_in, 16)
            pool.dma_start(ident[:], consts[:, K_ID:K_ID + P]).then_inc(consts_in, 16)
            pool.dma_start(rot[:], consts[:, K_ROT:K_ROT + P]).then_inc(consts_in, 16)
            pool.dma_start(c01[:].rearrange("p a b -> p (a b)"), consts[:, K_C01:K_C01 + P]).then_inc(consts_in, 16)
            pool.dma_start(pe2[:, 0, :], pe_k).then_inc(consts_in, 16)
            pool.dma_start(pe2[:, 1, :], pe_v).then_inc(consts_in, 16)
            pool.dma_start(w2s[:, 0], w2_k).then_inc(consts_in, 16)
            pool.dma_start(w2s[:, 1], w2_v).then_inc(consts_in, 16)
            pool.dma_start(b2s[:], b2).then_inc(consts_in, 16)
            pool.wait_ge(mean_ready, 1)
            pool.dma_start(wgf[:], w_gate).then_inc(wg_in, 16)
            pool.dma_start(kcs[:], consts[:, K_CK:K_CK + 2 * T].rearrange("p (a t) -> p a t", a=2)).then_inc(kcs_in, 16)
            pool.dma_start(ccs[:], consts[0:DH, K_CC:K_CC + 2 * NC].rearrange("p (a t) -> p a t", a=2)).then_inc(kcs_in, 16)
            pool.dma_start(w1s[:], w1_k).then_inc(w1_in, 16)

            def store(n):
                pool.wait_ge(proj_taken, 2 + n + 1)
                pool.dma_start(proj[bass.ds(2 * n, 2)].rearrange("m p t -> p m t"), OS[:]).then_inc(stored, 16)

            def spread(dst, tile, rows, halves_to, semaphore, shift=0):
                for half in range(2):
                    src = proj[tile:tile + 2, 64 * half:64 * half + 64, :].rearrange("m p t -> p m t")
                    pool.dma_start(dst[halves_to:halves_to + DH, half::2, 0:T - shift],
                                   src[:, :, shift:T]).then_inc(semaphore, 16)

            with pool.Fori(0, A1 // 2) as i:
                for par in range(2):
                    store(2 * i + par)
            pool.wait_ge(stored, 16 * A1)
            spread(Kb, TILE_KS, DH, 0, kraw_in)
            spread(Kb, TILE_KW, DH, DH, kraw_in)
            for b, tile in enumerate((TILE_VS, TILE_VW)):
                pool.dma_start(Vst[:, b], proj[tile:tile + 2].rearrange("m p t -> p m t")).then_inc(vst_in, 16)
            spread(KD, TILE_KC, DH, 0, kd_in)
            spread(KD, TILE_KC, DH, DH, kd_in, shift=1)
            store(A1)
            store(A1 + 1)
            pool.wait_ge(hid_done, 1)
            pool.dma_start(w1s[:], w1_v).then_inc(w1_in, 16)
            spread(KD, TILE_VC, DH, 0, kd_in)
            spread(KD, TILE_VC, DH, DH, kd_in, shift=1)

            def query(c, g):
                m, r0 = g // 2, DH * (g % 2)
                tile = proj[bass.ds(TILE_Q + 2 * c + m, 1)]
                for base in (0, DH):
                    for dst, lo_, hi_, row in ((Qb, 0, DH, 0), (Qs, 0, 8, 8), (Qs, 8, 16, 0)):
                        pool.dma_start(dst[base + lo_:base + hi_, g:g + 1, :],
                                       tile[:, r0 + row:r0 + row + hi_ - lo_, :].rearrange("m p t -> p m t")).then_inc(q_in, 16)

            pool.wait_ge(glog_done, 1)
            pool.memset(Qs[:], 0.0).then_inc(qs_clear, 1)
            pool.wait_ge(qs_clear, 1)
            pool.wait_ge(stored, 16 * (A1 + 1))
            for g in range(GRP):
                query(0, g)
            pool.wait_ge(hid_done, 2)
            pool.dma_start(qcs[:], consts[:, K_CQ:K_CQ + 2 * T].rearrange("p (a t) -> p a t", a=2)).then_inc(qcs_in, 16)
            store(A1 + 2)
            store(A1 + 3)
            pool.wait_ge(vc_ready, 1)
            pool.wait_ge(stored, 16 * (A1 + A2))

            def group(kv, last):
                pool.wait_ge(v_done, 1 + 32 * kv)
                pool.tensor_copy(VG[:], Vb[:, :, :, bass.ds(kv * DH, DH)])
                pool.tensor_copy(VCG[:], VC[:, kv, :]).then_inc(vg_ready, 1)
                for g in range(GRP):
                    if not last:
                        pool.wait_ge(q_ready, GRP * kv + g + 2)
                        pool.wait_ge(q_in, 96 * (GRP * kv + g + 1))
                        query(kv + 1, g)
                    if last and g == GRP - 1:
                        pool.wait_ge(stored, 16 * (A1 + A2 + 13))
                        fetch(0)
                    store(A1 + A2 + GRP * kv + g)

            def fetch(h):
                pool.dma_start(LF[:], proj[TILE_HF + h]).then_inc(f_ld, 16)
                pool.dma_start(LG[:], proj[TILE_HG + h]).then_inc(g_ld, 16)
                pool.dma_start(LI[:], proj[TILE_HI + h]).then_inc(i_ld, 16)
                pool.dma_start(LQ[:], proj[TILE_HQ + h]).then_inc(q_ld, 16)

            with pool.Fori(0, KV - 1) as kv:
                group(kv, False)
            group(KV - 1, True)

            pool.wait_ge(o_ready, 1 + H_B)
            pool.dma_start(lmask[:].rearrange("p l t -> p (l t)"), level_mask).then_inc(lm_in, 16)
            pool.wait_ge(stored, 16 * (A1 + A2 + B_))
            n_c = A1 + A2 + B_
            with pool.Fori(0, H_A - 1) as h:
                store(n_c + 2 * h)
                pool.wait_ge(fin_ready, h + 1)
                pool.wait_ge(sg_ready, h + 1)
                pool.wait_ge(itr_done, h + 1)
                fetch(h + 1)
                store(n_c + 2 * h + 1)
            store(n_c + 2 * H_A - 2)
            store(n_c + 2 * H_A - 1)
            pool.wait_ge(stored, 16 * (n_c + 2 * H_A))
            pool.wait_ge(ot_done, 8)

            def merge_gates(c, par):
                pool.dma_start(MG[:, par, 0:2, :], proj[bass.ds(TILE_MA + 2 * c, 2)].rearrange("m p t -> p m t")).then_inc(mg_in[par], 16)
                pool.dma_start(MG[:, par, 2:4, :], proj[bass.ds(TILE_MB + 2 * c, 2)].rearrange("m p t -> p m t")).then_inc(mg_in[par], 16)

            merge_gates(0, 0)
            with pool.Fori(0, D_ // 2 - 1) as i:
                pool.wait_ge(ms_ready, 1 + 2 * i)
                merge_gates(2 * i + 1, 1)
                pool.wait_ge(ms_ready, 1 + 2 * i + 1)
                merge_gates(2 * i + 2, 0)
            pool.wait_ge(ms_ready, 1 + D_ - 2)
            merge_gates(D_ - 1, 1)
            pool.wait_ge(unit_done, 1 + U_E)
            pool.wait_ge(ms_ready, 1 + D_)
            for g in range(4):
                pool.dma_start(HX[:, 4 * g:4 * g + 4, :],
                               x_t[4 * g:4 * g + 4].rearrange("k p t -> p k t")).then_inc(hx_in, 16)
            pool.wait_ge(mean_ready, 3)
            pool.memset(FFA[:], 0.0).then_inc(ffn_clear, 1)

        def split_hi(act, u0, per, i, s):
            s = s + AHEAD
            u = u0 + per * i + s
            r = (u0 + s) % RING
            if not (isinstance(u, int) and u < RING):
                act.wait_ge(unit_done, 1 + u - RING + 1)
            act.wait_ge(landed[r], 16 * ((u0 + s) // RING + (per // RING) * i + 1))
            nc.scalar.activation(whi[r][:], raw[r][:], ACT.Copy).then_inc(hi_ready, 1)

        def split_lo(dve, u0, per, i, s):
            s = s + AHEAD
            r = (u0 + s) % RING
            dve.wait_ge(hi_ready, u0 + per * i + s + 1)
            nc.vector.tensor_tensor(wlo[r][:], raw[r][:], whi[r][:].bitcast(F32), ALU.subtract).then_inc(lo_ready, 1)

        @block.tensor
        def _(pe):
            def mm(o, l, r, start, stop):
                return nc.tensor.matmul(o, l, r, start=start, stop=stop, skip_group_check=True)

            def unit(u0, per, i, s, hi, lo, k0, bank, first, last, side=None, split=None):
                if split is not None:
                    pe.wait_ge(act_lo, split)
                u = u0 + per * i + s
                r = (u0 + s) % RING
                pe.wait_ge(lo_ready, u + 1)
                for j in range(KU):
                    for m in range(2):
                        w = slice(j * CH + m * P, j * CH + m * P + P)
                        o = ps[:, bank + m, :]
                        mm(o, whi[r][:, w], hi[:, k0 + j, :], first and j == 0, False)
                        mm(o, whi[r][:, w], lo[:, k0 + j, :], False, False)
                        done = mm(o, wlo[r][:, w], hi[:, k0 + j, :], False, last and j == KU - 1)
                    if j == KU - 1:
                        done.then_inc(unit_done, 1)
                    if side is not None:
                        side(4 * s + j)

            def proj_chunk(u0, per, i, s0, n, side=None):
                par = (s0 // 4) % 2
                pe.wait_ge(proj_taken, 1 + n)
                for q in range(4):
                    unit(u0, per, i, s0 + q, XH, XL, 4 * q, 2 * par, q == 0, q == 3, side)

            def token_sums(src, n):
                pe.wait_ge(ssum_ready, n)
                for c in range(NT):
                    o = mm(ps[:, 6, c:c + 1], src[:, c * P:c * P + P], ones[:, 0:1], True, True)
                o.then_inc(mean_ready, 1)

            def row(diag, bank, n):
                pe.wait_ge(diag_ready, n)
                mm(ps[:, bank, :], ones[:], diag[:].rearrange("p c t -> p (c t)"), True, True).then_inc(row_done, 1)

            def two_in_turns(u0, base):
                for s in range(8):
                    unit(u0, 0, 0, s, XH, XL, 4 * (s // 2), 2 * (s % 2), s < 2, s >= 6,
                         split=base + 4 * (s // 2) + 4)

            pe.wait_ge(ones_ok, 1)
            two_in_turns(U_A1, 0)
            token_sums(XS[:, 0, :], 1)
            row(DG, 4, 1)
            with pe.Fori(1, A1 // 2) as i:
                for par in range(2):
                    proj_chunk(U_A1, 8, i, 4 * par, 2 * i + par)

            def prepare(t):
                if t in (8, 10, 12, 14):
                    kv = (t - 8) // 2
                    if kv == 0:
                        pe.wait_ge(kraw_in, 64)
                        pe.wait_ge(row_ready, 1)
                        pe.wait_ge(consts_ok, 1)
                    if kv >= 2:
                        pe.wait_ge(k_ready, kv - 1)
                    mm(ps[:, 4 + kv % 2, :], rot[:], Kb[:, kv, :], True, True).then_inc(krot_done, 1)
                if t in (16, 18, 20, 22):
                    g = (t - 16) // 2
                    b, m = g // 2, g % 2
                    if g == 0:
                        pe.wait_ge(vst_in, 32)
                        pe.wait_ge(gates_ready, 1)
                    if g >= 2:
                        pe.wait_ge(v_ready, g - 1)
                    for kb in range(NT):
                        o = nc.tensor.transpose(ps[:, 6 + g % 2, kb * P:kb * P + P], Vst[:, b, m, kb * P:kb * P + P], ident[:])
                    o.then_inc(vt_done, 1)
                for x, t0 in ((0, 24), (1, 42)):
                    if t0 <= t < t0 + 8:
                        if t == t0:
                            pe.wait_ge(blocks_ready, x + 1)
                            pe.wait_ge(w1_in, 16 * (x + 1))
                            pe.wait_ge(k_ready, KV)
                            pe.wait_ge(gelu_done, x)
                        for jm in range(4 * (t - t0), 4 * (t - t0) + 4):
                            m, j = jm // 16, jm % 16
                            o = mm(ps[:, 4, m * 128:m * 128 + KV * CB], w1s[:, j, m * P:m * P + P],
                                   Rb[:, j].rearrange("p a b -> p (a b)"), j == 0, j == 15)
                        if t == t0 + 7:
                            o.then_inc(hid_done, 1)
                    if t == t0 + 9:
                        pe.wait_ge(gelu_done, x + 1)
                        for m in range(2):
                            o = mm(ps[0:DH, 5, 0:KV * CB], w2s[:, x, m, :], HG[:, m, :], m == 0, m == 1)
                        o.then_inc(cmp_done, 1)
                if t == 36:
                    pe.wait_ge(cmp_biased, 1)
                    pe.wait_ge(v_ready, 4)
                    mm(ps[0:DH, 6, 0:KV * NC], rot[0:DH, 0:DH], cmpo[:].rearrange("p a b -> p (a b)"), True, True).then_inc(crot_done, 1)
                if t == 54:
                    pe.wait_ge(cmp_biased, 2)
                    for kv in range(KV):
                        o = nc.tensor.transpose(ps[0:NC, 7, kv * DH:kv * DH + DH], cmpo[:, kv, :], ident[0:DH, 0:DH])
                    o.then_inc(vct_done, 1)
                if t < 4:
                    if t == 0:
                        pe.wait_ge(wg_lo_ok, 1)
                        pe.wait_ge(std_ready, 1)
                    for k in range(4 * t, 4 * t + 4):
                        for a, (l, r) in enumerate(((wgh, XH), (wgh, XL), (wgl, XH))):
                            o = mm(ps[0:48, 6, :], l[:, k, :], r[:, k, :], k == 0 and a == 0, k == DT - 1 and a == 2)
                    if t == 3:
                        o.then_inc(glog_done, 1)
                if t == 6:
                    pe.wait_ge(glog_out, 1)
                    for c in range(NT):
                        o = nc.tensor.transpose(ps[:, 7, c * 48:c * 48 + 48], GL[:, c * P:c * P + P], ident[0:48, 0:48])
                    o.then_inc(glog_turned, 1)

            for c in range(A2):
                proj_chunk(U_A2, 0, 0, 4 * c, A1 + c, prepare)

            pe.wait_ge(q_ready, 1)
            with pe.Fori(0, KV) as kv:
                for g in range(GRP):
                    hd = GRP * kv + g

                    def head(t, hd=hd, kv=kv, g=g):
                        t -= 16 * g
                        k = t - 3
                        if k == 0:
                            pe.wait_ge(kc_ready, 1)
                            pe.wait_ge(exp_done, 1 + 9 * hd)
                            pe.wait_ge(q_ready, hd + 2)
                            mm(ps[:, 4, 0:NT * NC], identb[:], cmaskb[:], True, False)
                            for tt in range(NT):
                                o = mm(ps[:, 4, tt * NC:tt * NC + NC], QR[0:DH, 0, tt * P:tt * P + P], KC[:, kv, :], False, tt == NT - 1)
                            o.then_inc(s_done, 1)
                        if 1 <= k <= 8:
                            b, tt = (k - 1) % 2, (k - 1) // 2
                            n = P * (tt + 1)
                            if k >= 2:
                                pe.wait_ge(exp_done, 1 + 9 * hd + k - 1)
                            bank = ps[:, 4 + k % 2, :]
                            mm(bank[:, 0:n], QR[:, b, tt * P:tt * P + P], Kb[:, kv, 0:n], True, False)
                            mm(bank[:, n - P:n], identb[:], maskb[:], False, True).then_inc(s_done, 1)
                        k = t - 5
                        if 0 <= k <= 8:
                            pe.wait_ge(p_ready, 9 * hd + k + 1)
                            pe.wait_ge(pt_ready, 1 + 9 * hd + k)
                            if k == 0:
                                for tt in range(NT):
                                    o = nc.tensor.transpose(ps[0:NC, 6, tt * P:tt * P + P], PC[:, tt, :], ident[:])
                            else:
                                for kb in range((k - 1) // 2 + 1):
                                    o = nc.tensor.transpose(ps[:, 6, kb * P:kb * P + P], Pb[:, k % 2, kb * P:kb * P + P], ident[:])
                            o.then_inc(t_done, 1)
                        k = t - 7
                        if 1 <= k <= 8:
                            b, tt = (k - 1) % 2, (k - 1) // 2
                            pe.wait_ge(pt_ready, 1 + 9 * hd + k + 1)
                            if k == 1 and g == 0:
                                pe.wait_ge(vg_ready, kv + 1)
                            if k == 1:
                                pe.wait_ge(o_ready, 1 + hd)
                            o = ps[:, 7, tt * DH:tt * DH + DH]
                            if b == 0:
                                mm(o, PCT[:, tt * P:tt * P + P], VCG[:], True, False)
                            for kb in range(tt + 1):
                                last = mm(o, PT[:, k % 2, kb * P:kb * P + P], VG[:, b, kb, :],
                                          False, b == 1 and kb == tt)
                            last.then_inc(v_done, 1)

                    proj_chunk(U_B, 16, kv, 4 * g, A1 + A2 + hd, head)

            n_c = A1 + A2 + B_
            pe.wait_ge(o_ready, 1 + H_B)
            with pe.Fori(0, H_A) as h:
                def recur(t, h=h):
                    if t == 2:
                        pe.wait_ge(i_ld, 16 * (h + 1))
                        pe.wait_ge(ostd_ready, 1 + h)
                        for c in range(NT):
                            o = nc.tensor.transpose(ps[:, 7, c * P:c * P + P], LI[:, c * P:c * P + P], ident[:])
                        o.then_inc(itr_done, 1)
                    lev = (t - 4) // 3
                    if t == 4 + 3 * lev and 0 <= lev < LEVELS:
                        if lev == 0:
                            pe.wait_ge(q_ld, 16 * (h + 1))
                            pe.wait_ge(f_ready, h + 1)
                        else:
                            pe.wait_ge(qk_ready, 7 * h + lev)
                        if lev < 2:
                            pe.wait_ge(att_taken, 1 + 8 * h)
                        else:
                            pe.wait_ge(att_taken, 1 + 8 * h + lev - 1)
                        for c in range(NT):
                            cs = slice(c * P, c * P + P)
                            if lev == 0:
                                o = mm(ps[:, 4, cs], KF[:, cs], LQ[:, cs], True, True)
                            else:
                                hs = slice(c * P // 2, (c + 1) * P // 2)
                                o = mm(ps[:, 4 + lev % 2, hs], KT[:, lev % 2, cs], QT[:, lev % 2, hs], True, True)
                        o.then_inc(lev_done, 1)
                    if t == 26:
                        pe.wait_ge(oa_ready, 1 + h)
                        pe.wait_ge(fin_ready, h + 1)
                        for c in range(NT - 1):
                            o = nc.tensor.transpose(ps[:, 6, c * P:c * P + P], KE[:, c * P:c * P + P], ident[:])
                        o.then_inc(ktr_done, 1)
                    if t == 28:
                        pe.wait_ge(ktok_ready, h + 1)
                        pe.wait_ge(itok_ready, h + 1)
                        for c in range(NT - 1):
                            o = mm(ps[:, 7, c * P:c * P + P], KETOK[:, c, :], ITOK[:, c, :], True, True)
                        o.then_inc(g_done, 1)
                    if t == 30:
                        pe.wait_ge(st_ready, h + 1)
                        pe.wait_ge(att_taken, 1 + 8 * h + 8)
                        for c in range(NT):
                            o = ps[:, 6, c * P:c * P + P]
                            if c:
                                mm(o, ST[:, c - 1, :], QE[:, c * P:c * P + P], True, False)
                            last = mm(o, ITOK[:, c, :], ATT[:, c, :], c == 0, True)
                        last.then_inc(ro_done, 1)
                    if t == 31:
                        pe.wait_ge(osq_ready, h + 1)
                        mm(ps[:, 7, :], ones[:], OSQ[:], True, True).then_inc(omean_done, 1)

                for par in range(2):
                    proj_chunk(U_C, 8, h, 4 * par, n_c + 2 * h + par, recur)

            def turn_output(f0):
                for f in range(f0, f0 + 4):
                    if f0:
                        pe.wait_ge(act_lo, DT + 8 + f - 3)
                    if f == 2:
                        pe.wait_ge(oa_ready, 1 + H_A)
                    for tt in range(NT):
                        o = nc.tensor.transpose(ps[:, 4 + f % 4, tt * P:tt * P + P], otok[:, tt, f * P:f * P + P], ident[:])
                    o.then_inc(ot_done, 1)

            def both(i, half, first=False):
                if not first:
                    pe.wait_ge(blk_taken, 1 + 2 * i + half)
                for q in range(4):
                    hi, lo = (OAH, OAL) if q < 2 else (OBH, OBL)
                    unit(U_D, 8, i, 4 * half + q, hi, lo, 4 * (q % 2), 4 * half + 2 * (q // 2), q % 2 == 0, q % 2 == 1,
                         split=DT + 4 * q + 4 if first and half == 0 else None)
                    if first and half == 0 and q == 0:
                        turn_output(4)

            pe.wait_ge(ostd_ready, 1 + H_A)
            turn_output(0)
            pe.wait_ge(proj_taken, 2 + n_c + C_)
            both(0, 0, first=True)
            both(0, 1, first=True)
            with pe.Fori(1, D_ // 2) as i:
                for half in range(2):
                    both(i, half)
            def output(i, half, first=False):
                pe.wait_ge(blk_taken, 1 + D_ + 2 * i + half)
                for q in range(4):
                    unit(U_E, 8, i, 4 * half + q, XH, XL, 4 * q, 2 * half, q == 0, q == 3,
                         split=DT + 16 + 4 * q + 4 if first else None)

            output(0, 0, first=True)
            output(0, 1)
            with pe.Fori(1, E_ // 2) as i:
                for half in range(2):
                    output(i, half)
            token_sums(SACC[:], 1 + E_)
            row(DG2, 7, 2)
            j0 = D_ + E_

            def gate_up(u0, per, i, s0, half, job):
                pe.wait_ge(blk_taken, 1 + job)
                for q in range(8):
                    unit(u0, per, i, s0 + q, XH, XL, 4 * (q % 4), 4 * half + 2 * (q // 4), q % 4 == 0, q % 4 == 3)

            def down(u0, per, i, s0, half, job, parity, tiles):
                pe.wait_ge(hid_lo, 1 + tiles - 2)
                for c in range(8):
                    pe.wait_ge(blk_taken, 1 + job + c)
                    r = (u0 + s0 + c) % RING
                    pe.wait_ge(lo_ready, u0 + per * i + s0 + c + 1)
                    for j in range(KU):
                        place = 2 * parity + j if j < 2 else 2 + j
                        if c == 0 and j == 2:
                            pe.wait_ge(hid_lo, 1 + tiles)
                        for m in range(2):
                            w = slice(j * CH + m * P, j * CH + m * P + P)
                            o = ps[:, 4 * half + 2 * (c % 2) + m, :]
                            mm(o, whi[r][:, w], HH[:, place, :], j == 0, False)
                            mm(o, whi[r][:, w], HL[:, place, :], False, False)
                            last = mm(o, wlo[r][:, w], HH[:, place, :], False, j == KU - 1)
                    last.then_inc(unit_done, 1)

            two_in_turns(U_G, DT + 32)
            pe.wait_ge(row_ready, 2)
            token_sums(MIX[:, 0, :], 2 + E_)
            row(DG2, 7, 3)
            pe.wait_ge(row_ready, 3)
            gate_up(U_G, 0, 0, 8, 1, j0 + 1)
            with pe.Fori(0, (PARTS - 1) // 2) as i:
                for half in range(2):
                    job = j0 + 2 + 20 * i + 10 * half
                    gate_up(U_G1, 48, i, 24 * half, half, job)
                    down(U_G1, 48, i, 24 * half + 8, 1 - half, job + 1, half, 4 * (2 * i + half) + 4)
                    gate_up(U_G1, 48, i, 24 * half + 16, half, job + 9)
            down(U_H, 0, 0, 0, 0, j0 + 2 + 10 * (PARTS - 1), 0, FT)
            token_sums(SACC2[:], 2 + E_ + 8)
            row(DG3, 7, 4)

        @block.scalar
        def _(act):
            act_fn = nc.scalar.activation

            def rounded(src, gain, k, base):
                act_fn(XH[:, k, :], src[:, k, :], ACT.Identity, scale=col(gain, k)).then_inc(act_hi, 1)

            def root(n):
                act.wait_ge(mean_ready, n)
                act_fn(cstat[:, 0, :], ps[:, 6, 0:NT], ACT.Sqrt, bias=eps[:, 0:1], scale=1.0 / D).then_inc(std_ready, 1)

            def row_out(n, dst, bank):
                act.wait_ge(row_done, n)
                act_fn(dst[:], ps[:, bank, :], ACT.Copy).then_inc(row_ready, 1)

            act.wait_ge(vec_in, 16)
            act.wait_ge(ones_ok, 2)
            for g in range(DT // KU):
                for k in range(KU * g, KU * g + KU):
                    act.wait_ge(x_in[k // 2], 16)
                    rounded(XS, V_PRE, k, 0)
                for u in (2 * g, 2 * g + 1):
                    split_hi(act, 0, 0, 0, u - AHEAD)
                for k in range(KU * g, KU * g + KU):
                    act.wait_ge(act_lo, k + 1)
                    act_fn(XS[:, k, :], XS[:, k, :], ACT.Square).then_inc(sq_ready, 1)
            for s in (5, 6, 7):
                split_hi(act, U_A1, 0, 0, s)
            act.wait_ge(lb_shifted, 1)
            act_fn(lbt[:, 0:2, :], lbt[:, 0:2, :], ACT.Exp).then_inc(lb_exp, 1)
            root(1)
            row_out(1, RSTD, 4)

            act.wait_ge(wg_in, 16)
            act_fn(wgh[:], wgf[:], ACT.Copy).then_inc(wg_hi_ok, 1)
            with act.Fori(1, A1 // 2) as i:
                for s in range(8):
                    split_hi(act, U_A1, 8, i, s)
            for s in range(4 * A2):
                split_hi(act, U_A2, 0, 0, s)
                if s == 1:
                    act.wait_ge(glog_done, 1)
                    act_fn(GL[:], ps[0:48, 6, :], ACT.Copy).then_inc(glog_out, 1)
                if s == 2:
                    act.wait_ge(glog_turned, 1)
                    for c in range(NT):
                        o = act_fn(gates[:, c, :], ps[:, 7, c * 48:c * 48 + 48], ACT.Sigmoid, scale=rtok[:, c:c + 1])
                    o.then_inc(gates_ready, 1)
                if s in (4, 5):
                    for g in (2 * (s - 4), 2 * (s - 4) + 1):
                        act.wait_ge(vt_done, g + 1)
                        act_fn(Vb[:, g // 2, :, (g % 2) * P:(g % 2) * P + P],
                               ps[:, 6 + g % 2, :].rearrange("p (a b) -> p a b", a=NT), ACT.Copy).then_inc(v_ready, 1)
                if s in (8, 12):
                    x = (s - 8) // 4
                    act.wait_ge(hid_done, x + 1)
                    for m in range(2):
                        o = act_fn(HG[:, m, :], ps[:, 4, m * 128:m * 128 + KV * CB], ACT.Gelu_apprx_tanh,
                                   bias=col((V_B1K, V_B1V)[x], m))
                    o.then_inc(gelu_done, 1)
                    act.wait_ge(cmp_done, x + 1)
                    if x:
                        act.wait_ge(kc_ready, 1)
                    act_fn(cmpo[:, :, 0:CB], ps[0:DH, 5, 0:KV * CB].rearrange("p (a b) -> p a b", a=KV),
                           ACT.Identity, bias=b2s[:, x:x + 1]).then_inc(cmp_biased, 1)
                if s == 13:
                    act.wait_ge(vct_done, 1)
                    act_fn(VC[:].rearrange("p a b -> p (a b)"), ps[0:NC, 7, 0:KV * DH], ACT.Copy).then_inc(vc_ready, 1)

            with act.Fori(0, KV) as kv:
                for g in range(GRP):
                    hd = GRP * kv + g

                    def exps(k):
                        act.wait_ge(max_ready, 9 * hd + k + 1)
                        if k == 0:
                            act_fn(PC[:], PC[:], ACT.Exp).then_inc(exp_done, 1)
                            return
                        act.wait_ge(t_done, 1 + 9 * hd + max(k - 1, 0))
                        n = P * ((k - 1) // 2 + 1)
                        act_fn(Pb[:, k % 2, 0:n], ps[:, 4 + k % 2, 0:n], ACT.Exp, bias=negmax[:, k % 2:k % 2 + 1],
                               accum_out=expsum[:, k % 2:k % 2 + 1]).then_inc(exp_done, 1)

                    def turned(k):
                        act.wait_ge(t_done, 1 + 9 * hd + k + 1)
                        act.wait_ge(v_done, 1 + 8 * hd + max(k - 2, 0))
                        if k == 0:
                            act_fn(PCT[:], ps[0:NC, 6, :], ACT.Copy).then_inc(pt_ready, 1)
                            return
                        n = P * ((k - 1) // 2 + 1)
                        act_fn(PT[:, k % 2, 0:n], ps[:, 6, 0:n], ACT.Copy).then_inc(pt_ready, 1)

                    split_hi(act, U_B, 16, kv, 4 * g)
                    exps(0)
                    split_hi(act, U_B, 16, kv, 4 * g + 1)
                    exps(1)
                    for k in (2, 3, 4):
                        exps(k)
                        turned(k - 2)
                    split_hi(act, U_B, 16, kv, 4 * g + 2)
                    for k in (5, 6, 7, 8):
                        exps(k)
                        turned(k - 2)
                    split_hi(act, U_B, 16, kv, 4 * g + 3)
                    turned(7)
                    turned(8)

            with act.Fori(0, H_A) as h:
                def decays(lev):
                    w = 1 << (lev - 1)
                    act.wait_ge(px_ready, 8 * h + lev)
                    if lev == 1:
                        act.wait_ge(ln_done, h + 1)
                    act_fn(flat(EQ, w), halves(LP, w)[1], ACT.Exp)
                    act_fn(flat(EK, w), halves(LX, w)[0], ACT.Exp).then_inc(dec_done, 1)

                split_hi(act, U_C, 8, h, 0)
                act.wait_ge(f_ld, 16 * (h + 1))
                act_fn(SIG[:], LF[:], ACT.Sigmoid).then_inc(sig_done, 1)
                act.wait_ge(g_ld, 16 * (h + 1))
                act_fn(SGM[:], LG[:], ACT.Sigmoid).then_inc(sgm_done, 1)
                act.wait_ge(f_ready, h + 1)
                act_fn(LP[:], SIG[:], ACT.Ln).then_inc(ln_done, 1)
                act.wait_ge(itr_done, h + 1)
                act_fn(ITOK[:].rearrange("p a b -> p (a b)"), ps[:, 7, :], ACT.Copy).then_inc(itok_ready, 1)
                decays(1)
                split_hi(act, U_C, 8, h, 1)
                decays(2)
                split_hi(act, U_C, 8, h, 2)
                decays(3)
                decays(4)
                split_hi(act, U_C, 8, h, 3)
                decays(5)
                split_hi(act, U_C, 8, h, 4)
                decays(6)
                split_hi(act, U_C, 8, h, 5)
                decays(7)
                act.wait_ge(px_ready, 8 * h + 8)
                act_fn(EB[:], LP[:], ACT.Exp)
                act_fn(EX[:], LX[:], ACT.Exp).then_inc(fin_exp, 1)
                split_hi(act, U_C, 8, h, 6)
                act.wait_ge(ktr_done, h + 1)
                act_fn(KETOK[:].rearrange("p a b -> p (a b)"), ps[:, 6, 0:3 * P], ACT.Copy).then_inc(ktok_ready, 1)
                split_hi(act, U_C, 8, h, 7)
                act.wait_ge(ro_done, h + 1)
                act.wait_ge(oa_ready, 1 + h)
                act_fn(OSQ[:], ps[:, 6, :], ACT.Square).then_inc(osq_ready, 1)
                act.wait_ge(omean_done, h + 1)
                act_fn(ORS[:], ps[:, 7, :], ACT.Sqrt, bias=eps[:, 0:1], scale=1.0 / P).then_inc(ostd_ready, 1)

            act.wait_ge(oa_ready, 1 + H_A)
            for f in range(8):
                act_fn(OAH[:, f, :], OAF[:, f, :], ACT.Copy).then_inc(act_hi, 1)
            for f in range(8):
                act.wait_ge(ot_done, f + 1)
                act_fn(OBH[:, f, :], ps[:, 4 + f % 4, :], ACT.Copy).then_inc(act_hi, 1)
            with act.Fori(0, D_ // 2) as i:
                for half in range(2):
                    for q in range(4):
                        split_hi(act, U_D, 8, i, 4 * half + q)
                        if q == 0:
                            act.wait_ge(mg_in[half], 32 * (i + 1))
                            act_fn(MG[:, half], MG[:, half], ACT.Sigmoid).then_inc(mg_ready, 1)
                    act.wait_ge(ms_ready, 1 + 2 * i + half + 1)
                    act_fn(XH[:, bass.ds(4 * i + 2 * half, 2), :], MS[:], ACT.Copy).then_inc(act_hi, 2)
            with act.Fori(0, E_ // 2) as i:
                for half in range(2):
                    for q in range(4):
                        split_hi(act, U_E, 8, i, 4 * half + q)
                    act.wait_ge(blk_taken, 1 + D_ + 2 * i + half + 2)
                    act_fn(SQ2[:], MIX[:, bass.ds(4 * i + 2 * half, 2), :], ACT.Square).then_inc(pair_sq, 1)
            root(2)
            row_out(2, RS1, 7)
            for k in range(DT):
                act.wait_ge(h_ready, k + 1)
                rounded(HX, V_PREF, k, DT + 32)
                act_fn(MIX[:, k, :], HX[:, k, :], ACT.Square).then_inc(sq_ready, 1)
                if k in (5, 9, 13):
                    split_hi(act, U_G, 0, 0, (k - 5) // 4)
            for s in range(3, 8):
                split_hi(act, U_G, 0, 0, s)
            root(3)
            row_out(3, RS2, 7)

            j0 = D_ + E_

            def gate_up(u0, per, i, s0, half, job, place, pair):
                value = HV[:, place:place + 2, :]
                for q in range(8):
                    if pair is not first:
                        split_hi(act, u0, per, i, s0 + q)
                    if q == (7 if pair is first else 3):
                        act.wait_ge(gate_ready, pair + 1)
                        act_fn(value, value, ACT.Silu).then_inc(silu_ready, 1)
                act.wait_ge(blk_taken, 1 + job + 2)
                act_fn(HH[:, place:place + 2, :], value, ACT.Copy).then_inc(hid_hi, 1)

            first = 0
            gate_up(U_G, 0, 0, 0, 0, j0, 0, first)
            gate_up(U_G, 0, 0, 8, 1, j0 + 1, 4, 1)
            with act.Fori(0, (PARTS - 1) // 2) as i:
                for half in range(2):
                    job = j0 + 2 + 20 * i + 10 * half
                    pair = 2 + 4 * i + 2 * half
                    gate_up(U_G1, 48, i, 24 * half, half, job, 2 * (1 - half), pair)
                    for q in range(8):
                        split_hi(act, U_G1, 48, i, 24 * half + 8 + q)
                    gate_up(U_G1, 48, i, 24 * half + 16, half, job + 9, 4, pair + 1)
            for c in range(8):
                if U_H + c + AHEAD < U_END:
                    split_hi(act, U_H, 0, 0, c)
                act.wait_ge(blk_taken, 1 + j0 + 2 + 10 * (PARTS - 1) + c + 2)
                if c:
                    act.wait_ge(ssum_ready, E_ + c)
                act_fn(SQ3[:], FFA[:, 2 * c:2 * c + 2, :], ACT.Square).then_inc(pair_sq, 1)
            act.wait_ge(mean_scaled, 1)
            act_fn(cstat[:, 0, :], cstat[:, 1, :], ACT.Sqrt, bias=eps[:, 0:1], scale=1.0 / D).then_inc(std_ready, 1)
            row_out(4, RS3, 7)

        @block.vector
        def _(dve):
            tt, ts, stt = nc.vector.tensor_tensor, nc.vector.tensor_scalar, nc.vector.scalar_tensor_tensor
            MUL, ADD, SUB, MAX = ALU.mult, ALU.add, ALU.subtract, ALU.max

            def then():
                dve.drain()

            dve.memset(ones[:], 1.0).then_inc(ones_ok, 1)
            dve.memset(eps[:], EPS).then_inc(ones_ok, 1)
            dve.wait_ge(vec_in, 16)

            def take(u_end, par, n):
                dve.wait_ge(unit_done, 1 + u_end)
                if not (isinstance(n, int) and n == 0):
                    dve.wait_ge(stored, 16 * n)
                tt(OS[:], ps[:, 2 * par:2 * par + 2, :], RSTD[:].unsqueeze(1).to_broadcast([P, 2, T]), MUL).then_inc(proj_taken, 1)

            def rest_of(src, gain, k, base):
                dve.wait_ge(act_hi, base + k + 1)
                stt(XL[:, k, :], src[:, k, :], col(gain, k), XH[:, k, :].bitcast(F32), MUL, SUB).then_inc(act_lo, 1)

            def add_up(sq):
                n = DT // 2
                while n:
                    then()
                    o = tt(sq[:, 0:n, :], sq[:, 0:n, :], sq[:, n:2 * n, :], ADD)
                    n //= 2
                o.then_inc(ssum_ready, 1)

            def diagonal(n, diag, factor=None):
                dve.wait_ge(std_ready, n)
                r = rtok if factor is None else factor
                dve.reciprocal(cstat[:, 2, :], cstat[:, 0, :])
                then()
                if factor is None:
                    dve.tensor_copy(rtok[:], cstat[:, 2, :])
                else:
                    tt(cstat[:, 2, :], cstat[:, 2, :], factor[:], MUL)
                    then()
                tt(diag[:], ident[:].unsqueeze(1).to_broadcast([P, NT, P]),
                   cstat[:, 2, :].unsqueeze(2).to_broadcast([P, NT, P]), MUL).then_inc(diag_ready, 1)

            for g in range(DT // KU):
                for k in range(KU * g, KU * g + KU):
                    rest_of(XS, V_PRE, k, 0)
                for u in (2 * g, 2 * g + 1):
                    split_lo(dve, 0, 0, 0, u - AHEAD)
            for s in (5, 6):
                split_lo(dve, U_A1, 0, 0, s)
            dve.wait_ge(sq_ready, DT)
            add_up(XS)
            split_lo(dve, U_A1, 0, 0, 7)
            dve.wait_ge(consts_in, 144)
            dve.tensor_copy(maskb[:], cload[:, 0:P])
            dve.tensor_copy(cmaskb[:], cload[:, P:2 * P])
            dve.tensor_copy(identb[:], ident[:])
            l0, l1 = vec[:, V_L0:V_L0 + H_A], vec[:, V_L1:V_L1 + H_A]
            tt(lbt[:, 2, :], l0, l1, MAX)
            then()
            tt(lbt[:, 0, :], l0, lbt[:, 2, :], SUB)
            tt(lbt[:, 1, :], l1, lbt[:, 2, :], SUB).then_inc(lb_shifted, 1)
            dve.memset(cmpo[:], 0.0).then_inc(consts_ok, 1)
            diagonal(1, DG)
            dve.wait_ge(row_ready, 1)
            take(U_A1 + 8, 0, 0)
            take(U_A1 + 8, 1, 1)
            dve.wait_ge(lb_exp, 1)
            tt(lbt[:, 1, :], lbt[:, 0, :], lbt[:, 1, :], ADD)
            then()
            dve.reciprocal(lbt[:, 1, :], lbt[:, 1, :])
            then()
            tt(lb[:], lbt[:, 0, :], lbt[:, 1, :], MUL)
            then()
            ts(olb[:], lb[:], -1.0, 1.0, MUL, ADD)

            dve.wait_ge(wg_hi_ok, 1)
            tt(wgl[:], wgf[:], wgh[:].bitcast(F32), SUB).then_inc(wg_lo_ok, 1)
            with dve.Fori(1, A1 // 2) as i:
                for s in range(8):
                    split_lo(dve, U_A1, 8, i, s)
                    if s % 4 == 3:
                        take(U_A1 + 8 * i + s + 1, s // 4, 2 * i + s // 4)

            def blocks(x):
                dve.wait_ge(kd_in, 64 * (x + 1))
                if x:
                    dve.wait_ge(hid_done, 1)
                for kv in range(KV):
                    for jh in range(2):
                        o = tt(Rb[:, 8 * jh:8 * jh + 8, kv, :],
                               KD[:, kv, 16 * jh:16 * jh + 16 * CB].rearrange("p (n s) -> p s n", s=16)[:, 0:16:2, :],
                               pe2[:, x, 8 * jh:8 * jh + 8].unsqueeze(2).to_broadcast([P, 8, CB]), ADD)
                o.then_inc(blocks_ready, 1)

            for s in range(4 * A2):
                split_lo(dve, U_A2, 0, 0, s)
                if s in (2, 3):
                    if s == 2:
                        dve.wait_ge(kcs_in, 32)
                    for kv in (2 * s - 4, 2 * s - 3):
                        dve.wait_ge(krot_done, kv + 1)
                        bank = ps[:, 4 + kv % 2, :]
                        tt(bank, bank, kcs[:, 1, :], MUL)
                        tt(Kb[:, kv, :], Kb[:, kv, :], kcs[:, 0, :], MUL)
                        then()
                        tt(Kb[:, kv, :], Kb[:, kv, :], bank, ADD).then_inc(k_ready, 1)
                if s in (4, 9):
                    blocks((s - 4) // 5)
                if s == 9:
                    dve.wait_ge(crot_done, 1)
                    bank = ps[0:DH, 6, 0:KV * NC].rearrange("p (a b) -> p a b", a=KV)
                    cc, sc = (ccs[:, a, :].unsqueeze(1).to_broadcast([DH, KV, NC]) for a in range(2))
                    tt(bank, bank, sc, MUL)
                    tt(KC[:], cmpo[:], cc, MUL)
                    then()
                    tt(KC[:], KC[:], bank, ADD).then_inc(kc_ready, 1)
                if s % 4 == 3:
                    take(U_A2 + s + 1, (s // 4) % 2, A1 + s // 4)
            dve.wait_ge(qcs_in, 16)
            dve.wait_ge(gates_ready, 1)
            dve.wait_ge(vc_ready, 1)
            dve.wait_ge(v_ready, 4)
            dve.memset(rsum[:], 0.0).then_inc(q_ready, 1)

            dve.memset(QR[:], 0.0)
            then()
            with dve.Fori(0, KV) as kv:
                for g in range(GRP):
                    hd = GRP * kv + g

                    def maxima(k):
                        dve.wait_ge(s_done, 9 * hd + k + 1)
                        if k:
                            n = P * ((k - 1) // 2 + 1)
                            nc.vector.tensor_reduce(negmax[:, k % 2:k % 2 + 1], ps[:, 4 + k % 2, 0:n], AX.X, MAX,
                                                    negate=True).then_inc(max_ready, 1)
                            return
                        s = ps[:, 4, 0:NT * NC].rearrange("p (a b) -> p a b", a=NT)
                        nc.vector.tensor_reduce(cstat[:, 0, :], s, AX.X, MAX)
                        then()
                        tt(PC[:], s, cstat[:, 0, :].unsqueeze(2).to_broadcast([P, NT, NC]), SUB).then_inc(max_ready, 1)

                    def weigh(k):
                        dve.wait_ge(exp_done, 1 + 9 * hd + k + 1)
                        if k:
                            b, t_ = (k - 1) % 2, (k - 1) // 2
                            n = P * (t_ + 1)
                            r = slice(k % 2, k % 2 + 1)
                            dve.reciprocal(rsum[:, r], expsum[:, r])
                            then()
                            ts(rsum[:, r], rsum[:, r], gates[:, t_, bass.ds(3 * hd + 1 + b, 1)], None, MUL)
                            then()
                            ts(Pb[:, k % 2, 0:n], Pb[:, k % 2, 0:n], rsum[:, r], None, MUL).then_inc(p_ready, 1)
                            return
                        nc.vector.tensor_reduce(cstat[:, 1, :], PC[:], AX.X, ADD)
                        then()
                        tt(PC[:], PC[:], c01[:], MUL)
                        dve.reciprocal(cstat[:, 1, :], cstat[:, 1, :])
                        then()
                        tt(cstat[:, 2, :], cstat[:, 1, :], gates[:, :, bass.ds(3 * hd, 1)].rearrange("p a b -> p (a b)"), MUL)
                        then()
                        tt(PC[:], PC[:], cstat[:, 2, :].unsqueeze(2).to_broadcast([P, NT, NC]), MUL).then_inc(p_ready, 1)

                    split_lo(dve, U_B, 16, kv, 4 * g)
                    dve.wait_ge(q_in, 96 * (hd + 1))
                    tt(Qs[:, g, :], Qs[:, g, :], qcs[:, 1, :], MUL)
                    tt(Qb[:, g, :], Qb[:, g, :], qcs[:, 0, :], MUL)
                    then()
                    for b, rows in enumerate((slice(0, DH), slice(DH, P))):
                        o = tt(QR[rows, b, :], Qb[rows, g, :], Qs[rows, g, :], ADD)
                    o.then_inc(q_ready, 1)
                    maxima(0)
                    weigh(0)
                    split_lo(dve, U_B, 16, kv, 4 * g + 1)
                    maxima(1)
                    for k in (2, 3, 4):
                        maxima(k)
                        weigh(k - 1)
                    split_lo(dve, U_B, 16, kv, 4 * g + 2)
                    for k in (5, 6, 7, 8):
                        maxima(k)
                        weigh(k - 1)
                    split_lo(dve, U_B, 16, kv, 4 * g + 3)
                    weigh(8)
                    dve.wait_ge(v_done, 1 + 8 * hd + 8)
                    dve.tensor_copy(otok[:, :, bass.ds(hd * DH, DH)],
                                    ps[:, 7, 0:NT * DH].rearrange("p (a b) -> p a b", a=NT)).then_inc(o_ready, 1)
                    take(U_B + 16 * kv + 4 * g + 4, g % 2, A1 + A2 + hd)

            dve.memset(KT[:], 0.0)
            dve.memset(ATT[:], 0.0)
            then()
            def finish(h):
                dve.wait_ge(ostd_ready, 1 + h + 1)
                dve.reciprocal(ORS[:], ORS[:])
                then()
                stt(OSQ[:], ps[:, 6, :], vec[:, bass.ds(V_AN + h, 1)], ORS[:], MUL, MUL)
                then()
                tt(OAF[:, h, :], OSQ[:], SG[:], MUL).then_inc(oa_ready, 1)

            def recurrence_head(h, first):
                def decayed(lev):
                    w = 1 << (lev - 1)
                    if lev >= 3:
                        dve.wait_ge(lev_done, 8 * h + lev - 1)
                    dve.wait_ge(dec_done, 7 * h + lev)
                    b = lev % 2
                    tt(flat(QT[:, b], w), halves(LQ, w)[1], flat(EQ, w), MUL)
                    tt(halves(KT[:, b], w)[0], halves(KF, w)[0], flat(EK, w), MUL).then_inc(qk_ready, 1)
                    (p_lo, p_up), (x_lo, x_up) = halves(LP, w), halves(LX, w)
                    shape = [P, T // (2 * w), w]
                    tt(x_lo, x_lo, p_up[:, :, w - 1:w].to_broadcast(shape), ADD)
                    then()
                    tt(p_up, p_up, p_lo[:, :, w - 1:w].to_broadcast(shape), ADD).then_inc(px_ready, 1)

                def keep(lev):
                    dve.wait_ge(lev_done, 8 * h + lev + 1)
                    if lev == 0:
                        dve.wait_ge(lm_in, 16)
                    dve.memset(waited[:, lev:lev + 1], 0.0)
                    m = lmask[:, lev, :].bitcast(U32)
                    if lev == 0:
                        to, m, new = ATT[:], m.unsqueeze(1).to_broadcast([P, NT, P]), ps[:, 4, :].rearrange("p (a b) -> p a b", a=NT)
                    else:
                        w, n = 1 << (lev - 1), P >> lev
                        to = ATT[:].rearrange("p c (b h w) -> p c b h w", h=2, w=w)[:, :, :, 1, :]
                        m = m[:, 0:P // 2].rearrange("p (b w) -> p b w", w=w).unsqueeze(1).to_broadcast([P, NT, n, w])
                        new = ps[:, 4 + lev % 2, 0:T // 2].rearrange("p (c b w) -> p c b w", c=NT, w=w)
                    nc.vector.copy_predicated(to, m, new).then_inc(att_taken, 1)

                split_lo(dve, U_C, 8, h, 0)
                dve.memset(LX[:], 0.0).then_inc(px_ready, 1)
                dve.wait_ge(sig_done, h + 1)
                ts(SIG[:], SIG[:], olb[:, bass.ds(h, 1)], lb[:, bass.ds(h, 1)], MUL, ADD)
                then()
                ts(KF[:], SIG[:], -1.0, 1.0, MUL, ADD).then_inc(f_ready, 1)
                if not first:
                    finish(h - 1)
                    then()
                dve.wait_ge(sgm_done, h + 1)
                tt(SG[:], SGM[:], LG[:], MUL).then_inc(sg_ready, 1)
                dve.wait_ge(q_ld, 16 * (h + 1))
                decayed(1)
                split_lo(dve, U_C, 8, h, 1)
                keep(0)
                decayed(2)
                keep(1)
                split_lo(dve, U_C, 8, h, 2)
                decayed(3)
                keep(2)
                decayed(4)
                split_lo(dve, U_C, 8, h, 3)
                keep(3)
                decayed(5)
                take(U_C + 8 * h + 4, 0, A1 + A2 + B_ + 2 * h)
                split_lo(dve, U_C, 8, h, 4)
                keep(4)
                decayed(6)
                keep(5)
                split_lo(dve, U_C, 8, h, 5)
                decayed(7)
                keep(6)
                dve.wait_ge(fin_exp, h + 1)
                tt(QE[:], LQ[:], EB[:], MUL)
                tt(KE[:], KF[:], EX[:], MUL).then_inc(fin_ready, 1)
                split_lo(dve, U_C, 8, h, 6)
                then()
                keep(7)
                split_lo(dve, U_C, 8, h, 7)
                dve.wait_ge(g_done, h + 1)
                dve.tensor_copy(ST[:, 0, :], ps[:, 7, 0:P])
                for c in (1, 2):
                    then()
                    o = stt(ST[:, c, :], ST[:, c - 1, :], EB[:, c * P + P - 1:c * P + P], ps[:, 7, c * P:c * P + P], MUL, ADD)
                o.then_inc(st_ready, 1)
                take(U_C + 8 * h + 8, 1, A1 + A2 + B_ + 2 * h + 1)

            recurrence_head(0, True)
            with dve.Fori(1, H_A) as h:
                recurrence_head(h, False)
            finish(H_A - 1)

            for f in range(8):
                dve.wait_ge(act_hi, DT + f + 1)
                tt(OAL[:, f, :], OAF[:, f, :], OAH[:, f, :].bitcast(F32), SUB).then_inc(act_lo, 1)
            then()
            for f in range(8):
                dve.wait_ge(act_hi, DT + 8 + f + 1)
                tt(OBL[:, f, :], ps[:, 4 + f % 4, :], OBH[:, f, :].bitcast(F32), SUB).then_inc(act_lo, 1)
            with dve.Fori(0, D_ // 2) as i:
                for half in range(2):
                    for q in range(4):
                        split_lo(dve, U_D, 8, i, 4 * half + q)
                    then()
                    dve.wait_ge(mg_ready, 2 * i + half + 1)
                    dve.wait_ge(unit_done, 1 + U_D + 8 * i + 4 * half + 4)
                    dve.wait_ge(act_hi, DT + 16 + 4 * i + 2 * half)
                    tt(MT[:], MG[:, half, 0:2, :], ps[:, 4 * half:4 * half + 2, :], MUL)
                    tt(MS[:], MG[:, half, 2:4, :], ps[:, 4 * half + 2:4 * half + 4, :], MUL).then_inc(blk_taken, 1)
                    then()
                    tt(MS[:], MS[:], MT[:], ADD).then_inc(ms_ready, 1)
                    dve.wait_ge(act_hi, DT + 16 + 4 * i + 2 * half + 2)
                    f = bass.ds(4 * i + 2 * half, 2)
                    tt(XL[:, f, :], MS[:], XH[:, f, :].bitcast(F32), SUB).then_inc(act_lo, 2)

            def add_squares(total, sq, n):
                then()
                dve.wait_ge(pair_sq, n + 1)
                tt(total[:], total[:], sq[:, 0, :], ADD)
                then()
                tt(total[:], total[:], sq[:, 1, :], ADD).then_inc(ssum_ready, 1)

            dve.memset(SACC[:], 0.0)
            with dve.Fori(0, E_ // 2) as i:
                for half in range(2):
                    for q in range(4):
                        split_lo(dve, U_E, 8, i, 4 * half + q)
                    dve.wait_ge(unit_done, 1 + U_E + 8 * i + 4 * half + 4)
                    dve.tensor_copy(MIX[:, bass.ds(4 * i + 2 * half, 2), :], ps[:, 2 * half:2 * half + 2, :]).then_inc(blk_taken, 1)
                    add_squares(SACC, SQ2, 2 * i + half)
            diagonal(2, DG2)
            dve.wait_ge(row_ready, 2)
            dve.wait_ge(hx_in, 64)
            for k in range(DT + 2):
                then()
                if k < DT:
                    stt(TN2[:, k % 2, :], MIX[:, k, :], col(V_POST, k), RS1[:], MUL, MUL)
                if 1 <= k <= DT:
                    tt(HX[:, k - 1, :], HX[:, k - 1, :], TN2[:, (k - 1) % 2, :], ADD).then_inc(h_ready, 1)
                if k >= 2:
                    rest_of(HX, V_PREF, k - 2, DT + 32)
                if k in (8, 12, 16):
                    split_lo(dve, U_G, 0, 0, (k - 8) // 4)
            for s in (3, 4):
                split_lo(dve, U_G, 0, 0, s)
            dve.wait_ge(sq_ready, 2 * DT)
            add_up(MIX)
            for s in (5, 6, 7):
                split_lo(dve, U_G, 0, 0, s)
            diagonal(3, DG2)

            j0 = D_ + E_

            def gate_up(u0, per, i, s0, half, place, pair):
                value = HV[:, place:place + 2, :]
                for q in range(8):
                    if pair is not first:
                        split_lo(dve, u0, per, i, s0 + q)
                    if q == (7 if pair is first else 3):
                        if pair is first:
                            dve.wait_ge(row_ready, 3)
                        dve.wait_ge(unit_done, 1 + u0 + per * i + s0 + q + 1)
                        tt(value, ps[:, 4 * half:4 * half + 2, :], RS2[:].unsqueeze(1).to_broadcast([P, 2, T]), MUL).then_inc(gate_ready, 1)
                dve.wait_ge(unit_done, 1 + u0 + per * i + s0 + 8)
                dve.wait_ge(silu_ready, pair + 1)
                tt(value, value, ps[:, 4 * half + 2:4 * half + 4, :], MUL).then_inc(blk_taken, 1)
                then()
                dve.wait_ge(hid_hi, pair + 1)
                tt(HL[:, place:place + 2, :], value, HH[:, place:place + 2, :].bitcast(F32), SUB).then_inc(hid_lo, 2)

            def add_part(u_end, bank, c):
                then()
                dve.wait_ge(unit_done, 1 + u_end)
                tt(FFA[:, 2 * c:2 * c + 2, :], FFA[:, 2 * c:2 * c + 2, :], ps[:, bank:bank + 2, :], ADD).then_inc(blk_taken, 1)

            first = 0
            gate_up(U_G, 0, 0, 0, 0, 0, first)
            gate_up(U_G, 0, 0, 8, 1, 4, 1)
            dve.wait_ge(ffn_clear, 1)
            with dve.Fori(0, (PARTS - 1) // 2) as i:
                for half in range(2):
                    pair = 2 + 4 * i + 2 * half
                    gate_up(U_G1, 48, i, 24 * half, half, 2 * (1 - half), pair)
                    for c in range(8):
                        split_lo(dve, U_G1, 48, i, 24 * half + 8 + c)
                        add_part(U_G1 + 48 * i + 24 * half + 9 + c, 4 * (1 - half) + 2 * (c % 2), c)
                    gate_up(U_G1, 48, i, 24 * half + 16, half, 4, pair + 1)
            dve.memset(SACC2[:], 0.0)
            for c in range(8):
                if U_H + c + AHEAD < U_END:
                    split_lo(dve, U_H, 0, 0, c)
                add_part(U_H + c + 1, 2 * (c % 2), c)
                add_squares(SACC2, SQ3, E_ + c)
            dve.wait_ge(mean_ready, 4)
            tt(cstat[:, 1, :], ps[:, 6, 0:NT], rtok[:], MUL)
            then()
            tt(cstat[:, 1, :], cstat[:, 1, :], rtok[:], MUL).then_inc(mean_scaled, 1)
            diagonal(4, DG3, factor=rtok)
            dve.wait_ge(row_ready, 4)
            for k in range(DT + 1):
                then()
                if k < DT:
                    stt(FFA[:, k, :], FFA[:, k, :], col(V_POSTF, k), RS3[:], MUL, MUL)
                if k:
                    tt(FFA[:, k - 1, :], FFA[:, k - 1, :], HX[:, k - 1, :], ADD).then_inc(out_ready, 1)


def chunks(w, n):
    k = w.shape[0] // P
    return np.ascontiguousarray(w.reshape(k, P, n, CH).transpose(2, 1, 0, 3).reshape(n, P, k * CH))


def by_tile(v):
    return v.reshape(-1, P).T


def shape_constants():
    half = 8
    inv = np.float32(500000.0) ** (-np.arange(half, dtype=np.float32) * np.float32(2.0) / np.float32(16))

    def tables(pos, scale):
        ang = pos.astype(np.float32)[:, None] * inv[None, :]
        c, s = np.ones((DH, len(pos)), np.float32), np.zeros((DH, len(pos)), np.float32)
        c[0:half] = c[half:2 * half] = np.cos(ang).T
        s[0:half] = s[half:2 * half] = np.sin(ang).T
        return c * np.float32(scale), s * np.float32(scale)

    k = np.zeros((P, K_N), np.float32)
    k[:, K_ID:K_ID + P] = np.eye(P)
    for base in (0, DH):
        for i in range(half):
            k[base + half + i, K_ROT + base + i] = -1.0
            k[base + i, K_ROT + base + half + i] = 1.0
    q, c = np.arange(P)[:, None], np.arange(P)[None, :]
    k[:, K_DIAG:K_DIAG + P] = np.where(c > q, NEG, 0.0)
    t = q + P * np.arange(NT).repeat(NC)[None, :]
    n = np.tile(np.arange(NC), NT)[None, :]
    seen = (16 * n + CB <= t) & (n < CB)
    k[:, K_CM:K_CM + P] = np.where(seen, 0.0, NEG)
    k[:, K_C01:K_C01 + P] = seen
    flip = np.where(np.arange(DH) < half, -1.0, 1.0).astype(np.float32)[:, None]
    for at_, pos, scale in (((K_CQ, K_SQ), np.arange(T), DH ** -0.5), ((K_CK, K_SK), np.arange(T), 1.0),
                            ((K_CC, K_SC), np.arange(NC) * 16 + CB, 1.0)):
        for a, tab in zip(at_, tables(pos, scale)):
            k[0:DH, a:a + len(pos)] = k[DH:P, a:a + len(pos)] = tab
            if a == K_SQ:
                k[0:DH, a:a + len(pos)] = k[DH:P, a:a + len(pos)] = tab * flip
    masks = np.zeros((P, LEVELS, P), np.float32)
    masks[:, 0, :] = np.eye(P)
    s, j = np.arange(P)[:, None], np.arange(P // 2)[None, :]
    for lev in range(1, LEVELS):
        w = 1 << (lev - 1)
        masks[:, lev, 0:P // 2] = (s // (2 * w) == j // w) & (s % (2 * w) < w)
    return k, masks.reshape(P, LEVELS * P)


def kernel(**inputs):
    import concourse.bacc as bacc
    from concourse.bass_utils import run_bass_kernel_spmd

    a = {n: np.asarray(v) for n, v in inputs.items()}
    w_in = a["w_in"][0]
    kv = [w_in[:, 5120 + CH * j:5120 + CH * j + CH] for j in range(6)]
    consts, masks = shape_constants()
    arrays = {
        "x_t": np.ascontiguousarray(a["x"][0].T).reshape(DT, P, T),
        "w_a": chunks(np.concatenate(kv + [w_in[:, 4096:5120]], axis=1), A1 + A2),
        "w_b": chunks(w_in[:, 0:4096], B_),
        "w_c": chunks(w_in[:, 6704:10800], C_),
        "w_d": np.concatenate([chunks(a["w_proj_a"][0], D_), chunks(a["w_proj_b"][0], D_)], axis=2),
        "w_e": chunks(a["w_out"][0], E_),
        "w_g": np.concatenate([chunks(a["w_gate"][0], FF // CH), chunks(a["w_up"][0], FF // CH)], axis=2),
        "w_h": np.ascontiguousarray(a["w_down"][0].reshape(PARTS, KU, P, 8, CH).transpose(0, 2, 3, 1, 4)
                                    .reshape(PARTS, P, 8 * UN)),
        "w_gate": np.ascontiguousarray(w_in[:, 6656:6704].reshape(DT, P, 48).transpose(1, 0, 2)),
        "vecs": np.ascontiguousarray(np.concatenate([by_tile(v) for v in (
            a["pre_mix_g"][0], a["post_mix_g"][0], a["pre_ffn_g"][0], a["post_ffn_g"][0], a["a_norm_g"][0],
            a["lb_table"][0], a["lb_table"][1], a["cmp_b1_k"][0], a["cmp_b1_v"][0])], axis=1)),
        "consts": consts,
        "level_mask": masks,
    }
    for x in ("k", "v"):
        arrays["pe_" + x] = np.ascontiguousarray(a["cmp_pe_" + x][0].reshape(16, P).T)
    for x in ("k", "v"):
        arrays["w1_" + x] = np.ascontiguousarray(a["cmp_w1_" + x][0].reshape(16, P, CH).transpose(1, 0, 2))
    for x in ("k", "v"):
        arrays["w2_" + x] = np.ascontiguousarray(a["cmp_w2_" + x][0].reshape(2, P, DH).transpose(1, 0, 2))
    arrays["b2"] = np.ascontiguousarray(np.stack([a["cmp_b2_k"][0], a["cmp_b2_v"][0]], axis=1))

    nc = bacc.Bacc("TRN2", target_bir_lowering=False, num_devices=1)
    args = [nc.dram_tensor("in_" + n, v.shape, mybir.dt.from_np(v.dtype), kind="ExternalInput").ap()
            for n, v in arrays.items()]
    res = nc.dram_tensor("out_t", [DT, P, T], F32, kind="ExternalOutput").ap()
    hybrid_block(nc, *args, res)
    r = run_bass_kernel_spmd(nc, [{"in_" + n: v for n, v in arrays.items()}], core_ids=[0])
    return np.ascontiguousarray(r.results[0]["out_t"].reshape(D, T).T)[None]
```
